# Optimizing a Trainium2 kernel written in Bass

```python
import math
import jax, jax.numpy as jnp
from jax import lax
import numpy as np

D_MODEL = 1024
BATCH = 1
SEQ = 256
DEPTH = 1

CHUNK = 64
N_MIXERS = 3
PLE_DIM = 256
D_FF = 4 * D_MODEL
NORM_EPS = 1e-6
SSM_GROUP = 16
SSM_GROUPS = D_MODEL // SSM_GROUP
SSM_STATE = 64
DT_MIN = 1e-3
DT_MAX = 1e-1
CONV_WIDTH = 3
FOX_HEAD_DIM = 64
FOX_HEADS = D_MODEL // FOX_HEAD_DIM
Q_BLOCK = 128

N_SSM_LAYERS = len(range(0, DEPTH, N_MIXERS))
N_CONV_LAYERS = len(range(1, DEPTH, N_MIXERS))
N_FOX_LAYERS = len(range(2, DEPTH, N_MIXERS))


def rmsnorm(x, gain):
    xf = x.astype(jnp.float32)
    out = xf * lax.rsqrt(jnp.mean(xf * xf, axis=-1, keepdims=True) + NORM_EPS) * gain.astype(jnp.float32)
    return out.astype(x.dtype)

def s5_mixer(u, lam_re, lam_im, log_dt, b_re, b_im, c_re, c_im, d_skip, w_glu):
    f32 = jnp.float32
    bsz, seqlen, _ = u.shape
    uf = u.astype(f32)
    ug = uf.reshape(bsz, seqlen, SSM_GROUPS, SSM_GROUP)
    lr = lam_re.astype(f32)
    li = lam_im.astype(f32)
    dt = jnp.exp(log_dt.astype(f32))[:, None]
    mag = jnp.exp(lr * dt)
    ab_re = mag * jnp.cos(li * dt)
    ab_im = mag * jnp.sin(li * dt)
    nr = ab_re - 1.0
    ni = ab_im
    den = lr * lr + li * li
    coef_re = (nr * lr + ni * li) / den
    coef_im = (ni * lr - nr * li) / den
    br = b_re.astype(f32)
    bi = b_im.astype(f32)
    bb_re = coef_re[..., None] * br - coef_im[..., None] * bi
    bb_im = coef_re[..., None] * bi + coef_im[..., None] * br
    bu_re = jnp.einsum('blgh,gph->blgp', ug, bb_re)
    bu_im = jnp.einsum('blgh,gph->blgp', ug, bb_im)
    a_re = jnp.broadcast_to(ab_re, (1, seqlen, SSM_GROUPS, SSM_STATE))
    a_im = jnp.broadcast_to(ab_im, (1, seqlen, SSM_GROUPS, SSM_STATE))

    def combine(left, right):
        a1r, a1i, b1r, b1i = left
        a2r, a2i, b2r, b2i = right
        return (a2r * a1r - a2i * a1i,
                a2r * a1i + a2i * a1r,
                a2r * b1r - a2i * b1i + b2r,
                a2r * b1i + a2i * b1r + b2i)

    _, _, xs_re, xs_im = lax.associative_scan(combine, (a_re, a_im, bu_re, bu_im), axis=1)
    y = (jnp.einsum('blgp,ghp->blgh', xs_re, c_re.astype(f32))
         - jnp.einsum('blgp,ghp->blgh', xs_im, c_im.astype(f32)))
    y = y.reshape(bsz, seqlen, D_MODEL) + d_skip.astype(f32) * uf
    y = jax.nn.gelu(y).astype(u.dtype)
    a, g = jnp.split(y @ w_glu, 2, axis=-1)
    return a * jax.nn.sigmoid(g)

def short_conv_mixer(h, w_in, conv_w, w_out):
    b_gate, c_gate, v = jnp.split(h @ w_in, 3, axis=-1)
    z = c_gate * v
    rhs = conv_w[:, None, :].astype(z.dtype)
    conv = lax.conv_general_dilated(
        z, rhs, window_strides=(1,), padding=[(CONV_WIDTH - 1, 0)],
        dimension_numbers=('NWC', 'WIO', 'NWC'), feature_group_count=D_MODEL)
    return (b_gate * conv) @ w_out

def fox_mixer(h, w_in, b_f, w_out):
    f32 = jnp.float32
    bsz, seqlen, _ = h.shape
    proj = h @ w_in
    q, k, v, f_logit = jnp.split(proj, [D_MODEL, 2 * D_MODEL, 3 * D_MODEL], axis=-1)
    q = q.reshape(bsz, seqlen, FOX_HEADS, FOX_HEAD_DIM)
    k = k.reshape(bsz, seqlen, FOX_HEADS, FOX_HEAD_DIM)
    v = v.reshape(bsz, seqlen, FOX_HEADS, FOX_HEAD_DIM)
    log_f = jax.nn.log_sigmoid(f_logit.astype(f32) + b_f.astype(f32))
    cum = jnp.cumsum(log_f, axis=1).transpose(0, 2, 1)
    scale = FOX_HEAD_DIM ** -0.5
    outs = []
    for blk in range(seqlen // Q_BLOCK):
        q0 = blk * Q_BLOCK
        kv_len = q0 + Q_BLOCK
        s = jnp.einsum('bqhd,bkhd->bhqk', q[:, q0:kv_len], k[:, :kv_len]).astype(f32) * scale
        decay = cum[:, :, q0:kv_len, None] - cum[:, :, None, :kv_len]
        causal = (q0 + jnp.arange(Q_BLOCK))[:, None] >= jnp.arange(kv_len)[None, :]
        s = jnp.where(causal, s + decay, -jnp.inf)
        pr = jax.nn.softmax(s, axis=-1).astype(v.dtype)
        outs.append(jnp.einsum('bhqk,bkhd->bqhd', pr, v[:, :kv_len]))
    o = jnp.concatenate(outs, axis=1).reshape(bsz, seqlen, D_MODEL)
    return o @ w_out

def sqrelu_mlp(h, w1, w2):
    a = jax.nn.relu(h @ w1)
    return (a * a) @ w2

def first_inputs(seed: int = 0) -> dict:
    key = jax.random.key(seed)
    ks = jax.random.split(key, 26)
    f32 = jnp.float32
    nrm = lambda k, shape, s: jax.random.normal(k, shape, f32) * s
    gain = lambda k, shape: 1.0 + 0.05 * jax.random.normal(k, shape, f32)
    ns, nc, nf = N_SSM_LAYERS, N_CONV_LAYERS, N_FOX_LAYERS
    G, P, H = SSM_GROUPS, SSM_STATE, SSM_GROUP
    lam_im_init = jnp.broadcast_to(jnp.arange(P, dtype=f32) * math.pi, (ns, G, P))
    return {
        "x": nrm(ks[0], (BATCH, SEQ, D_MODEL), 1.0),
        "p": nrm(ks[1], (DEPTH, BATCH, SEQ, PLE_DIM), 1.0),
        "norm_mix": gain(ks[2], (DEPTH, D_MODEL)),
        "norm_ffn": gain(ks[3], (DEPTH, D_MODEL)),
        "norm_ple": gain(ks[4], (DEPTH, D_MODEL)),
        "norm_final": gain(ks[5], (D_MODEL,)),
        "ssm_lam_re": -0.5 + 0.01 * jax.random.normal(ks[6], (ns, G, P), f32),
        "ssm_lam_im": lam_im_init + 0.01 * jax.random.normal(ks[7], (ns, G, P), f32),
        "ssm_log_dt": jax.random.uniform(ks[8], (ns, G), f32, math.log(DT_MIN), math.log(DT_MAX)),
        "ssm_b_re": nrm(ks[9], (ns, G, P, H), (2 * H) ** -0.5),
        "ssm_b_im": nrm(ks[10], (ns, G, P, H), (2 * H) ** -0.5),
        "ssm_c_re": nrm(ks[11], (ns, G, H, P), (2 * P) ** -0.5),
        "ssm_c_im": nrm(ks[12], (ns, G, H, P), (2 * P) ** -0.5),
        "ssm_d": nrm(ks[13], (ns, D_MODEL), 1.0),
        "ssm_w_glu": nrm(ks[14], (ns, D_MODEL, 2 * D_MODEL), D_MODEL ** -0.5),
        "conv_w_in": nrm(ks[15], (nc, D_MODEL, 3 * D_MODEL), D_MODEL ** -0.5),
        "conv_w": nrm(ks[16], (nc, CONV_WIDTH, D_MODEL), CONV_WIDTH ** -0.5),
        "conv_w_out": nrm(ks[17], (nc, D_MODEL, D_MODEL), D_MODEL ** -0.5),
        "fox_w_in": nrm(ks[18], (nf, D_MODEL, 3 * D_MODEL + FOX_HEADS), D_MODEL ** -0.5),
        "fox_b_f": 3.0 + 0.5 * jax.random.normal(ks[19], (nf, FOX_HEADS), f32),
        "fox_w_out": nrm(ks[20], (nf, D_MODEL, D_MODEL), D_MODEL ** -0.5),
        "mlp_w1": nrm(ks[21], (DEPTH, D_MODEL, D_FF), D_MODEL ** -0.5),
        "mlp_w2": nrm(ks[22], (DEPTH, D_FF, D_MODEL), D_FF ** -0.5),
        "ple_w": nrm(ks[23], (DEPTH, PLE_DIM, D_MODEL), PLE_DIM ** -0.5),
        "ple_gate_w": nrm(ks[24], (DEPTH, D_MODEL, D_MODEL), D_MODEL ** -0.5),
    }

def first_block(x, p, norm_mix, norm_ffn, norm_ple, norm_final,
              ssm_lam_re, ssm_lam_im, ssm_log_dt, ssm_b_re, ssm_b_im, ssm_c_re, ssm_c_im,
              ssm_d, ssm_w_glu, conv_w_in, conv_w, conv_w_out, fox_w_in, fox_b_f, fox_w_out,
              mlp_w1, mlp_w2, ple_w, ple_gate_w):
    for i in range(DEPTH):
        kind, slot = i % N_MIXERS, i // N_MIXERS
        h = rmsnorm(x, norm_mix[i])
        if kind == 0:
            mix = s5_mixer(h, ssm_lam_re[slot], ssm_lam_im[slot], ssm_log_dt[slot],
                           ssm_b_re[slot], ssm_b_im[slot], ssm_c_re[slot], ssm_c_im[slot],
                           ssm_d[slot], ssm_w_glu[slot])
        elif kind == 1:
            mix = short_conv_mixer(h, conv_w_in[slot], conv_w[slot], conv_w_out[slot])
        else:
            mix = fox_mixer(h, fox_w_in[slot], fox_b_f[slot], fox_w_out[slot])
        x = x + mix
        x = x + sqrelu_mlp(rmsnorm(x, norm_ffn[i]), mlp_w1[i], mlp_w2[i])
        gate = jax.nn.sigmoid(rmsnorm(x, norm_ple[i]) @ ple_gate_w[i])
        x = x + (p[i] @ ple_w[i]) * gate
    return rmsnorm(x, norm_final)


DEPTH_2 = 2

GRID_W = 64
CTX_LEN = 256
HEAD_DIM = 64
BRANCH_WIDTH = D_MODEL // 2
FOURIER_GROUP_DIM = 64
FOURIER_GROUPS = BRANCH_WIDTH // FOURIER_GROUP_DIM
CONV_WIDTH_2 = BRANCH_WIDTH
CONV_KERNEL = 31
GQA_Q_HEADS = BRANCH_WIDTH // HEAD_DIM
GQA_GROUP = 4
GQA_KV_HEADS = GQA_Q_HEADS // GQA_GROUP
DIFF_QK_DIM = HEAD_DIM
DIFF_V_DIM = 2 * HEAD_DIM
DIFF_HEADS = BRANCH_WIDTH // DIFF_V_DIM
N_BRANCH = 4
FFN_HIDDEN = -(-8 * D_MODEL // (3 * 256)) * 256
ROPE_BASE = 10000.0
AXIS_ROT_DIM = HEAD_DIM // 2
EPS = 1e-6
LN_EPS = 1e-5

_IN_SIZES = (BRANCH_WIDTH,
             2 * CONV_WIDTH_2,
             GQA_Q_HEADS * HEAD_DIM,
             GQA_KV_HEADS * HEAD_DIM,
             GQA_KV_HEADS * HEAD_DIM,
             DIFF_HEADS * 2 * DIFF_QK_DIM,
             DIFF_HEADS * 2 * DIFF_QK_DIM,
             DIFF_HEADS * DIFF_V_DIM,
             N_BRANCH * D_MODEL)
IN_COLS = sum(_IN_SIZES)
SPLIT_IDX = tuple(int(v) for v in np.cumsum(_IN_SIZES)[:-1])


def rms_norm(x, g):
    x32 = x.astype(jnp.float32)
    y = x32 * lax.rsqrt(jnp.mean(x32 * x32, axis=-1, keepdims=True) + EPS)
    return (y * g.astype(jnp.float32)).astype(x.dtype)

def layer_norm(x, g, b):
    x32 = x.astype(jnp.float32)
    mu = jnp.mean(x32, axis=-1, keepdims=True)
    var = jnp.mean(jnp.square(x32 - mu), axis=-1, keepdims=True)
    y = (x32 - mu) * lax.rsqrt(var + LN_EPS)
    return (y * g.astype(jnp.float32) + b.astype(jnp.float32)).astype(x.dtype)

def modulate(h, shift, scale):
    return h * (1.0 + scale) + shift

def axial_rope_tables(n_rows):
    row = jnp.repeat(jnp.arange(n_rows, dtype=jnp.float32), GRID_W)
    col = jnp.tile(jnp.arange(GRID_W, dtype=jnp.float32), n_rows)
    inv = ROPE_BASE ** (-jnp.arange(0, AXIS_ROT_DIM, 2, dtype=jnp.float32) / AXIS_ROT_DIM)
    ang = jnp.concatenate([row[:, None] * inv, col[:, None] * inv], axis=-1)
    return jnp.cos(ang), jnp.sin(ang)

def rope(x, cos, sin):
    half = x.shape[-1] // 2
    x32 = x.astype(jnp.float32)
    x1, x2 = x32[..., :half], x32[..., half:]
    return jnp.concatenate([x1 * cos - x2 * sin, x2 * cos + x1 * sin], axis=-1).astype(x.dtype)

def fourier_mix(z):
    b, l, _ = z.shape
    zg = z.reshape(b, l, FOURIER_GROUPS, FOURIER_GROUP_DIM).astype(jnp.float32)
    f = jnp.fft.fft2(zg, axes=(1, 3), norm="ortho").real
    return f.reshape(b, l, BRANCH_WIDTH).astype(z.dtype)

def conformer_conv(z, w, bias, ln_g, ln_b):
    a, g = jnp.split(z, 2, axis=-1)
    u = a * jax.nn.sigmoid(g)
    pad = CONV_KERNEL // 2
    y = lax.conv_general_dilated(u, w[:, None, :].astype(u.dtype), window_strides=(1,),
                                 padding=[(pad, pad)], dimension_numbers=("NWC", "WIO", "NWC"),
                                 feature_group_count=CONV_WIDTH_2) + bias
    return jax.nn.silu(layer_norm(y, ln_g, ln_b))

def gqa_q(zq, g, cos, sin):
    b, l, _ = zq.shape
    q = rms_norm(zq.reshape(b, l, GQA_Q_HEADS, HEAD_DIM), g).transpose(0, 2, 1, 3)
    if cos is not None:
        q = rope(q, cos, sin)
    return q.reshape(b, GQA_KV_HEADS, GQA_GROUP, l, HEAD_DIM)

def gqa_kv(zk, zv, g, cos, sin):
    b, l, _ = zk.shape
    k = rms_norm(zk.reshape(b, l, GQA_KV_HEADS, HEAD_DIM), g).transpose(0, 2, 1, 3)
    v = zv.reshape(b, l, GQA_KV_HEADS, HEAD_DIM).transpose(0, 2, 1, 3)
    if cos is not None:
        k = rope(k, cos, sin)
    return k, v

def diff_q(zq, cos, sin):
    b, l, _ = zq.shape
    q = zq.reshape(b, l, DIFF_HEADS, 2, DIFF_QK_DIM).transpose(0, 2, 3, 1, 4)
    if cos is not None:
        q = rope(q, cos, sin)
    return q

def diff_kv(zk, zv, cos, sin):
    b, l, _ = zk.shape
    k = zk.reshape(b, l, DIFF_HEADS, 2, DIFF_QK_DIM).transpose(0, 2, 3, 1, 4)
    v = zv.reshape(b, l, DIFF_HEADS, DIFF_V_DIM).transpose(0, 2, 1, 3)
    if cos is not None:
        k = rope(k, cos, sin)
    return k, v

def gqa_attend(q, k, v):
    s = jnp.einsum("bhgqd,bhkd->bhgqk", q, k).astype(jnp.float32) * (HEAD_DIM ** -0.5)
    p = jax.nn.softmax(s, axis=-1).astype(v.dtype)
    return jnp.einsum("bhgqk,bhkd->bhgqd", p, v)

def diff_attend(q, k, v, lam):
    s = jnp.einsum("bhmqd,bhmkd->bhmqk", q, k).astype(jnp.float32) * (DIFF_QK_DIM ** -0.5)
    p = jax.nn.softmax(s, axis=-1)
    w = (p[:, :, 0] - lam * p[:, :, 1]).astype(v.dtype)
    return jnp.einsum("bhqk,bhkd->bhqd", w, v)

def sweep_query_blocks(fn, q):
    *lead, s, d = q.shape
    nb = s // Q_BLOCK
    qb = jnp.moveaxis(q.reshape(*lead, nb, Q_BLOCK, d), -3, 0)
    out = jnp.moveaxis(lax.map(fn, qb), 0, -3)
    return out.reshape(*out.shape[:-3], s, out.shape[-1])

def gqa_merge(o):
    b, _, _, l, d = o.shape
    return o.reshape(b, GQA_Q_HEADS, l, d).transpose(0, 2, 1, 3).reshape(b, l, GQA_Q_HEADS * d)

def diff_merge(o, g, lam_init):
    b, h, l, dv = o.shape
    o = rms_norm(o, g) * (1.0 - lam_init)
    return o.transpose(0, 2, 1, 3).reshape(b, l, h * dv)

def context_keys_values(pc, lp):
    k, v = gqa_kv(pc[3], pc[4], lp["k_norm"], None, None)
    kd, vd = diff_kv(pc[6], pc[7], None, None)
    return (k, v, kd, vd)

def mixer_stream(parts, lp, cos, sin, ctx_kv, lam, lam_init):
    zf, zconv, zgq, zgk, zgv, zdq, zdk, zdv, zgate = parts
    y_four = fourier_mix(zf) @ lp["w_four"]
    y_conv = conformer_conv(zconv, lp["conv_w"], lp["conv_b"], lp["conv_ln_g"], lp["conv_ln_b"]) @ lp["w_conv"]
    q = gqa_q(zgq, lp["q_norm"], cos, sin)
    k, v = gqa_kv(zgk, zgv, lp["k_norm"], cos, sin)
    qd = diff_q(zdq, cos, sin)
    kd, vd = diff_kv(zdk, zdv, cos, sin)
    if ctx_kv is None:
        o_gqa = gqa_attend(q, k, v)
        o_diff = diff_attend(qd, kd, vd, lam)
    else:
        kc, vc, kdc, vdc = ctx_kv
        k_all = jnp.concatenate([k, kc], axis=2)
        v_all = jnp.concatenate([v, vc], axis=2)
        kd_all = jnp.concatenate([kd, kdc], axis=3)
        vd_all = jnp.concatenate([vd, vdc], axis=2)
        o_gqa = sweep_query_blocks(lambda qb: gqa_attend(qb, k_all, v_all), q)
        o_diff = sweep_query_blocks(lambda qb: diff_attend(qb, kd_all, vd_all, lam), qd)
    y_gqa = gqa_merge(o_gqa) @ lp["w_gqa"]
    y_diff = diff_merge(o_diff, lp["diff_norm"], lam_init) @ lp["w_diff"]
    b, l, _ = zgate.shape
    gates = jax.nn.sigmoid(zgate.reshape(b, l, N_BRANCH, D_MODEL))
    ys = jnp.stack([y_four, y_conv, y_gqa, y_diff], axis=2)
    return jnp.sum(gates * ys, axis=2) @ lp["w_out"]

def swiglu(h, w1, w3, w2):
    return (jax.nn.silu(h @ w1) * (h @ w3)) @ w2

def second_inputs(seed: int = 0) -> dict:
    key = jax.random.key(seed)
    ks = iter(jax.random.split(key, 40))

    def nrm(shape, scale):
        return scale * jax.random.normal(next(ks), shape, jnp.float32)

    def gain(shape):
        return 1.0 + nrm(shape, 0.02)

    L = DEPTH_2
    return {
        "x": nrm((BATCH, SEQ, D_MODEL), 1.0),
        "c": nrm((BATCH, D_MODEL), 1.0),
        "ctx": nrm((BATCH, CTX_LEN, D_MODEL), 1.0),
        "c_ctx": nrm((D_MODEL,), 1.0),
        "w_ada": nrm((L, D_MODEL, 6 * D_MODEL), 0.5 * D_MODEL ** -0.5),
        "b_ada": nrm((L, 6 * D_MODEL), 0.02),
        "norm_mix": gain((L, D_MODEL)),
        "w_in": nrm((L, D_MODEL, IN_COLS), D_MODEL ** -0.5),
        "w_four": nrm((L, BRANCH_WIDTH, D_MODEL), BRANCH_WIDTH ** -0.5),
        "conv_w": nrm((L, CONV_KERNEL, CONV_WIDTH_2), CONV_KERNEL ** -0.5),
        "conv_b": nrm((L, CONV_WIDTH_2), 0.02),
        "conv_ln_g": gain((L, CONV_WIDTH_2)),
        "conv_ln_b": nrm((L, CONV_WIDTH_2), 0.02),
        "w_conv": nrm((L, CONV_WIDTH_2, D_MODEL), CONV_WIDTH_2 ** -0.5),
        "q_norm": gain((L, HEAD_DIM)),
        "k_norm": gain((L, HEAD_DIM)),
        "w_gqa": nrm((L, GQA_Q_HEADS * HEAD_DIM, D_MODEL), (GQA_Q_HEADS * HEAD_DIM) ** -0.5),
        "lam_q1": nrm((L, DIFF_QK_DIM), 0.1),
        "lam_k1": nrm((L, DIFF_QK_DIM), 0.1),
        "lam_q2": nrm((L, DIFF_QK_DIM), 0.1),
        "lam_k2": nrm((L, DIFF_QK_DIM), 0.1),
        "diff_norm": gain((L, DIFF_V_DIM)),
        "w_diff": nrm((L, DIFF_HEADS * DIFF_V_DIM, D_MODEL), (DIFF_HEADS * DIFF_V_DIM) ** -0.5),
        "w_out": nrm((L, D_MODEL, D_MODEL), D_MODEL ** -0.5),
        "norm_ffn": gain((L, D_MODEL)),
        "w_ffn1": nrm((L, D_MODEL, FFN_HIDDEN), D_MODEL ** -0.5),
        "w_ffn3": nrm((L, D_MODEL, FFN_HIDDEN), D_MODEL ** -0.5),
        "w_ffn2": nrm((L, FFN_HIDDEN, D_MODEL), FFN_HIDDEN ** -0.5),
        "final_norm": gain((D_MODEL,)),
    }

def second_block(x, c, ctx, c_ctx, w_ada, b_ada, norm_mix, w_in, w_four, conv_w, conv_b, conv_ln_g,
              conv_ln_b, w_conv, q_norm, k_norm, w_gqa, lam_q1, lam_k1, lam_q2, lam_k2, diff_norm,
              w_diff, w_out, norm_ffn, w_ffn1, w_ffn3, w_ffn2, final_norm):
    n_rows = x.shape[1] // GRID_W
    cos, sin = axial_rope_tables(n_rows)
    silu_c = jax.nn.silu(c)
    silu_cc = jax.nn.silu(c_ctx)
    for l in range(DEPTH_2):
        last = l == DEPTH_2 - 1
        lam_init = 0.8 - 0.6 * math.exp(-0.3 * l)
        lp = dict(w_four=w_four[l], conv_w=conv_w[l], conv_b=conv_b[l], conv_ln_g=conv_ln_g[l],
                  conv_ln_b=conv_ln_b[l], w_conv=w_conv[l], q_norm=q_norm[l], k_norm=k_norm[l],
                  w_gqa=w_gqa[l], diff_norm=diff_norm[l], w_diff=w_diff[l], w_out=w_out[l])
        mod_x = (silu_c @ w_ada[l] + b_ada[l])[:, None, :]
        sh_m, sc_m, g_m, sh_f, sc_f, g_f = jnp.split(mod_x, 6, axis=-1)
        mod_c = silu_cc @ w_ada[l] + b_ada[l]
        csh_m, csc_m, cg_m, csh_f, csc_f, cg_f = jnp.split(mod_c, 6, axis=-1)
        lam = (jnp.exp(jnp.sum(lam_q1[l].astype(jnp.float32) * lam_k1[l].astype(jnp.float32)))
               - jnp.exp(jnp.sum(lam_q2[l].astype(jnp.float32) * lam_k2[l].astype(jnp.float32)))
               + lam_init)
        hx = modulate(rms_norm(x, norm_mix[l]), sh_m, sc_m)
        hc = modulate(rms_norm(ctx, norm_mix[l]), csh_m, csc_m)
        px = jnp.split(hx @ w_in[l], SPLIT_IDX, axis=-1)
        pc = jnp.split(hc @ w_in[l], SPLIT_IDX, axis=-1)
        ctx_kv = context_keys_values(pc, lp)
        x = x + g_m * mixer_stream(px, lp, cos, sin, ctx_kv, lam, lam_init)
        if not last:
            ctx = ctx + cg_m * mixer_stream(pc, lp, None, None, None, lam, lam_init)
            ctx = ctx + cg_f * swiglu(modulate(rms_norm(ctx, norm_ffn[l]), csh_f, csc_f),
                                      w_ffn1[l], w_ffn3[l], w_ffn2[l])
        x = x + g_f * swiglu(modulate(rms_norm(x, norm_ffn[l]), sh_f, sc_f),
                             w_ffn1[l], w_ffn3[l], w_ffn2[l])
    return rms_norm(x, final_norm)


def setup_inputs(seed=0):
    out = dict(first_inputs(seed))
    for name, value in second_inputs(seed + 1).items():
        if name != "x":
            out[name + "_2"] = value
    return out


def reference(
    x, p, norm_mix, norm_ffn, norm_ple, norm_final, ssm_lam_re, ssm_lam_im, ssm_log_dt,
    ssm_b_re, ssm_b_im, ssm_c_re, ssm_c_im, ssm_d, ssm_w_glu, conv_w_in, conv_w, conv_w_out,
    fox_w_in, fox_b_f, fox_w_out, mlp_w1, mlp_w2, ple_w, ple_gate_w, c_2, ctx_2, c_ctx_2,
    w_ada_2, b_ada_2, norm_mix_2, w_in_2, w_four_2, conv_w_2, conv_b_2, conv_ln_g_2,
    conv_ln_b_2, w_conv_2, q_norm_2, k_norm_2, w_gqa_2, lam_q1_2, lam_k1_2, lam_q2_2, lam_k2_2,
    diff_norm_2, w_diff_2, w_out_2, norm_ffn_2, w_ffn1_2, w_ffn3_2, w_ffn2_2, final_norm_2,
):
    x = first_block(
        x, p, norm_mix, norm_ffn, norm_ple, norm_final, ssm_lam_re, ssm_lam_im, ssm_log_dt,
        ssm_b_re, ssm_b_im, ssm_c_re, ssm_c_im, ssm_d, ssm_w_glu, conv_w_in, conv_w, conv_w_out,
        fox_w_in, fox_b_f, fox_w_out, mlp_w1, mlp_w2, ple_w, ple_gate_w,
    )
    return second_block(
        x, c_2, ctx_2, c_ctx_2, w_ada_2, b_ada_2, norm_mix_2, w_in_2, w_four_2, conv_w_2,
        conv_b_2, conv_ln_g_2, conv_ln_b_2, w_conv_2, q_norm_2, k_norm_2, w_gqa_2, lam_q1_2,
        lam_k1_2, lam_q2_2, lam_k2_2, diff_norm_2, w_diff_2, w_out_2, norm_ffn_2, w_ffn1_2,
        w_ffn3_2, w_ffn2_2, final_norm_2,
    )


_drawn_inputs = setup_inputs


def setup_inputs(seed=0):
    import zlib

    import numpy as np

    out = dict(_drawn_inputs(seed))
    spreads = {}
    factors = {'norm_ple': 8.0,
     'ssm_lam_re': 8.0,
     'ssm_lam_im': 2.874,
     'ssm_log_dt': 2.889,
     'ssm_b_re': 3.976,
     'ssm_b_im': 3.963,
     'ssm_c_re': 4.088,
     'ssm_c_im': 3.996,
     'norm_mix_2': 8.0,
     'conv_b_2': 8.0,
     'conv_ln_g_2': 8.0,
     'conv_ln_b_2': 8.0,
     'q_norm_2': 8.0,
     'k_norm_2': 8.0,
     'lam_q1_2': 4.267,
     'lam_k1_2': 3.067,
     'lam_q2_2': 3.862,
     'lam_k2_2': 5.504,
     'diff_norm_2': 8.0,
     'norm_ffn_2': 6.947,
     'final_norm_2': 2.908}
    for name, (base, spread) in spreads.items():
        noise = np.random.default_rng([zlib.crc32(name.encode()), seed]).standard_normal(out[name].shape)
        drawn = base * np.exp(spread * noise) if base else spread * noise
        out[name] = __import__('jax').numpy.asarray(drawn.astype(out[name].dtype))
    for name, factor in factors.items():
        out[name] = (out[name] * factor).astype(out[name].dtype)
    return out
```

```python
from contextlib import ExitStack, contextmanager

import numpy as np

import concourse.bass as bass
from concourse import mybir

F32 = mybir.dt.float32
F32R = mybir.dt.float32r
I32 = mybir.dt.int32
ALU = mybir.AluOpType
ACT = mybir.ActivationFunctionType
AX_X = mybir.AxisListType.X

P = 128
D = 1024
KD = D // P
SEQ = 256
CTX = 256
EPS = 1e-6
LN_EPS = 1e-5

FF1 = 4096
GROUPS, GH, STATE = 64, 16, 64
CH = 8
NCH = SEQ // CH
PAIRS = GROUPS // 2

LAYERS = 2
BW = 512
TAPS = 31
FFN = 2816
NT = FFN // P

COL = dict(four=0, conv=512, gq=1536, gkv=2048, dq=2304, dk=2816, dv=3328, gate=3840)

V_BADA, V_NMIX, V_NFFN, V_NPLE, V_NFIN = 0, 96, 104, 112, 120
V_CONVW = 128
V_NMIX2, V_NFFN2, V_FIN2, V_CB, V_LG, V_LB, V_C, V_CC, V_DN = 384, 400, 416, 424, 432, 440, 448, 456, 464

C_ID, C_DFT, C_DIM, C_ROPE, C_EYE, C_END = 0, 128, 1152, 1408, 1536, 1552

RING = 4
SLOT = 2048


def shape_constants():
    c = np.zeros((P, C_END), np.float32)
    c[:, C_ID:C_ID + P] = np.eye(P)
    n = np.arange(SEQ)
    ang = 2 * np.pi * ((n[:, None] * n[None, :]) % SEQ) / SEQ
    dft = np.concatenate([np.cos(ang), np.sin(ang)], 1)
    c[:, C_DFT:C_DIM] = dft.reshape(2, P, 2 * SEQ).transpose(1, 0, 2).reshape(P, -1)
    m = np.arange(64)
    ang = 2 * np.pi * ((m[:, None] * m[None, :]) % 64) / 64
    norm = 1.0 / np.sqrt(SEQ * 64.0)
    for k, t in enumerate((np.cos(ang) * norm, -np.sin(ang) * norm)):
        for g in range(2):
            c[64 * g:64 * g + 64, C_DIM + P * k + 64 * g:C_DIM + P * k + 64 * g + 64] = t
    inv = np.float32(10000.0) ** (-np.arange(0, 32, 2, dtype=np.float32) / np.float32(32))
    tok = np.arange(SEQ)
    ang = np.concatenate([(tok // 64).astype(np.float32)[:, None] * inv,
                          (tok % 64).astype(np.float32)[:, None] * inv], 1)
    rope = np.concatenate([np.cos(ang), np.sin(ang)], 1).astype(np.float32)
    c[:, C_ROPE:C_EYE] = rope.reshape(2, P, 64).transpose(1, 0, 2).reshape(P, -1)
    c[0:GH, C_EYE:C_END] = np.eye(GH)
    return c


class Tally:

    def __init__(self, eng, sem):
        self.eng, self.sem, self.n, self.it, self.per = eng, sem, 0, None, 0

    def add(self, ins):
        ins.then_inc(self.sem, 1)
        self.n += 1
        return ins

    def value(self):
        return self.n if self.it is None else self.it * self.per + self.n

    def wait(self):
        self.eng.wait_ge(self.sem, self.value())

    @contextmanager
    def loop(self, it, trips, per):
        start = self.n
        self.it, self.per = it, per
        yield
        assert self.n - start == per, (self.n - start, per)
        self.it, self.per, self.n = None, 0, start + trips * per


class Phase:

    def __init__(self, name, n, body, src, kts, cols, units=1):
        self.name, self.n, self.body, self.src, self.units = name, n, body, src, units
        self.kts, self.cols = kts, cols


def repeat(eng, trips, body, peel_first=False, peel_last=False):
    lo, hi = (1 if peel_first else 0), (trips - 1 if peel_last else trips)
    if lo:
        body(0)
    if hi - lo >= 2:
        with eng.Fori(lo, hi) as it:
            body(it)
    elif hi - lo == 1:
        body(lo)
    if peel_last and trips > lo:
        body(trips - 1)


def build(nc, A, out):
    ctx = ExitStack()
    with ctx:
        base = [nc.sbuf_base]

        def at(name, shape, dt=F32, offset=None):
            off = base[0] if offset is None else offset
            off = (off + 31) // 32 * 32
            t = nc.alloc_sbuf_tensor_at(name, shape, dt, offset=off)
            size = 4
            for s in shape[1:]:
                size *= s
            if offset is None:
                base[0] = off + size
            return t, off, off + size

        def sb(name, shape, dt=F32):
            return at(name, shape, dt)[0]

        def sem(name):
            return ctx.enter_context(nc.semaphore(name))

        const = sb("const", [P, C_END])
        ones = sb("ones", [P, P])
        vecs = sb("vecs", [P, 512])
        mod = sb("mod", [P, LAYERS, 48, 2])
        msc = sb("msc", [P, LAYERS, 2, KD, 2])
        sc = sb("sc", [P, KD, 2])
        rs = sb("rs", [P, 4, 16])
        x = sb("x", [P, KD, SEQ + CTX])
        raw = sb("raw", [P, RING, SLOT])
        arena0 = base[0]
        xh = sb("xh", [P, KD, SEQ + CTX], F32R)
        xl = sb("xl", [P, KD, SEQ + CTX], F32R)
        wh = sb("wh", [P, 2, SLOT], F32R)
        wl = sb("wl", [P, 2, SLOT], F32R)
        arena1 = base[0]
        end = nc.sbuf_usable_end

        ident = const[:, C_ID:C_ID + P]

        gb = ctx.enter_context(nc.psum_tensor("gb", [P, 4, 512], F32))
        mb = ctx.enter_context(nc.psum_tensor("mb", [P, 4, 512], F32))

        def area(start, limit):
            o = [start]

            def take(name, shape, dt=F32):
                t, _, e = at(name, shape, dt, offset=o[0])
                assert e <= limit, (name, e, limit)
                o[0] = e
                return t
            take.mark = o
            return take

        part_a = area(arena0, arena0 + 20992)
        xnat = part_a("xnat", [P, 2, D])
        vnat = part_a("vnat", [P, 4, P])
        cnat = part_a("cnat", [P, 2, 4, P])
        lnat = part_a("lnat", [PAIRS, 4, P])
        sq32 = part_a("sq32", [NCH, D])
        part_b = area(arena0, arena0 + 20992)
        ksb = at("ksb", [GH, 32, P], F32, offset=part_b.mark[0])[0]
        F = part_b("F", [P, 2, 4, 2, CH, GH])
        tF = part_b("tF", [P, 8 * CH * GH])
        w1 = part_b("w1", [P, 4, 2, P])
        tE = part_b("tE", [P, 8 * (CH + 1) * GH])
        part_c = area(arena0 + 20992, arena0 + 32768)
        V = part_c("V", [P, NCH, 2, PAIRS])
        pwr = part_c("pwr", [P, CH, 2, PAIRS])
        tS = part_c("tS", [P, 3, 2, PAIRS])
        sst = part_c("sst", [NCH, 4, CH])
        part_d = area(arena0 + 32768, end)
        h32 = at("h32", [NCH, CH, D], F32, offset=part_d.mark[0])[0]
        E = part_d("E", [P, PAIRS, 2, CH + 1, GH])
        toep_at = part_d.mark[0]
        toep = part_d("toep", [P, GROUPS, P])
        hn = at("hn", [NCH, GROUPS, CH, GH], F32, offset=toep_at)[0]
        U = part_d("U", [P, GROUPS, NCH])
        s_at = part_d.mark[0]
        S = part_d("S", [P, NCH, 2, PAIRS])
        Bn = at("Bn", [P, 2, PAIRS, GH], F32, offset=s_at)[0]
        y_at = part_d.mark[0]
        ysb = part_d("ysb", [NCH, 2, CH, 8, GH])
        gainb = at("gainb", [NCH, D], F32, offset=y_at)[0]
        pw = part_d("pw", [P, CH + 1, 2, PAIRS])
        Bb = part_d("Bb", [P, 2, PAIRS, GH])
        Ct = part_d("Ct", [P, 2, PAIRS, GH])
        sm = part_d("sm", [P, 24, PAIRS])
        gl = part_d("gl", [P, 2, 4, SEQ])
        adat = part_d("adat", [2, 2, 256])
        Db = x[0:GH, 0:4, SEQ:SEQ + 256].rearrange("p k (g h) -> p k g h", h=GH)

        part_m = area(arena1, end)
        th = part_m("th", [P, 2, 512])
        pr = part_m("pr", [P, 2, 512])
        diag = part_m("diag", [P, 4, P])
        sqr = part_m("sqr", [P, 4, 512])
        arena2 = part_m.mark[0]
        hidh = part_m("hidh", [P, FF1 // P, SEQ], F32R)
        hidl = part_m("hidl", [P, FF1 // P, SEQ], F32R)
        part_p = area(arena2, end)
        pnat = part_p("pnat", [P, 2, SEQ])
        pth = part_p("pth", [P, 2, SEQ], F32R)
        ptl = part_p("ptl", [P, 2, SEQ], F32R)

        part_2 = area(arena1, end)
        th2 = part_2("th2", [P, 2, 1024])
        pr2 = part_2("pr2", [P, 2, 1024])
        over_th, over_pr = area(arena1, arena1 + 8192), area(arena1 + 8192, arena1 + 16384)
        cxnat = over_th("cxnat", [P, 2, D])
        PROBS = 6
        probs = at("probs", [P, PROBS, 512], F32, offset=arena1)[0]
        onat = at("onat", [P, 2, D], F32, offset=arena1)[0]
        sqr2 = over_pr("sqr2", [P, 4, 512])
        probt = at("probt", [P, 2, 512], F32, offset=arena1 + 12288)[0]

        dg2 = part_2("dg2", [P, 4, P])
        qkg = part_2("qkg", [P, LAYERS, 2, 64])
        lamb = part_2("lamb", [P, LAYERS])
        dgain = part_2("dgain", [P, LAYERS])
        st = part_2("st", [P, 4, 32])
        mx = part_2("mx", [P, 3, 8])
        hid_at = part_2.mark[0]
        mix = part_2("mix", [P, KD, SEQ + CTX])
        lamv = at("lamv", [P, 4, 2 * 64], F32, offset=hid_at)[0]
        brh = part_2("brh", [P, 4, SEQ + CTX], F32R)
        brl = part_2("brl", [P, 4, SEQ + CTX], F32R)
        z_at = part_2.mark[0]
        z1, z2, z3 = area(z_at, end), area(z_at, end), area(z_at, end)
        upad = z1("upad", [P, 4, 2, SEQ + TAPS - 1])
        cy = z1("cy", [P, 4, SEQ + CTX])
        after_conv = z1.mark[0]
        zf = z1("zf", [P, 4, BW])
        dft1 = z1("dft1", [P, 4, 2 * SEQ])
        gqT = z2("gqT", [P, 4, SEQ + CTX])
        gkT = z2("gkT", [P, SEQ + CTX])
        z2.mark[0] = after_conv
        gq = z2("gq", [P, 4, BW])
        gkv = z2("gkv", [P, 4, 256])
        tmp2 = z2("tmp2", [P, 2, 512])
        dq = z3("dq", [P, 4, BW])
        dk = z3("dk", [P, 4, BW])
        dqT = z3("dqT", [P, 4, SEQ + CTX])
        dkT = z3("dkT", [P, 4, SEQ + CTX])
        part_h = area(hid_at, end)
        FH = 12
        fhh = part_h("fhh", [P, FH, SEQ + CTX], F32R)
        fhl = part_h("fhl", [P, FH, SEQ + CTX], F32R)

        s_const = sem("const_loaded")
        s_nat = sem("naturals_loaded")
        s_h32 = sem("x_by_chunk_loaded")
        s_bd = sem("b_and_broadcasts_loaded")
        landed = [sem(f"landed{i}") for i in range(RING)]
        ada_used = sem("ada_block_used")
        s_ac = sem("ada_block_copied")
        s_at = sem("ada_block_transposed")
        hi_ready = sem("weights_hi_ready")
        w_ready = sem("weights_lo_ready")
        mm_done = sem("half_block_multiplied")
        drained = [sem(f"unit_drained{i}") for i in range(2)]
        s_act = sem("act_step")
        s_dve = sem("dve_step")
        s_pool = sem("pool_step")
        s_ones = sem("ones_set")
        s_pt = sem("params_transposed")
        s_xt = sem("x_transposed")
        s_params = sem("params_copied")
        s_mag = sem("magnitudes_ready")
        s_ang = sem("angles_ready")
        s_sin = sem("sines_ready")
        s_sc = sem("silu_c_ready")
        s_scx = sem("tanh_c_ready")
        s_adad = sem("ada_layer_done")
        s_pw = sem("powers_ready")
        s_pwr = sem("powers_reversed")
        s_F = sem("F_ready")
        s_w1t = sem("F_transposed")
        s_w1 = sem("w1_copied")
        s_w1u = sem("w1_used")
        s_E = sem("E_ready")
        s_ss = sem("squares_summed")
        s_h = sem("h_ready")
        s_U = sem("U_transposed")
        s_Uc = sem("U_copied")
        s_V = sem("V_multiplied")
        s_Vc = sem("V_copied")
        s_S = sem("states_ready")
        s_K = sem("K_multiplied")
        s_Kc = sem("K_copied")
        s_Kd = sem("K_with_skip")
        s_T = sem("toeplitz_placed")
        s_T0 = sem("toeplitz_zeroed")
        s_Y = sem("Y_multiplied")
        s_Yc = sem("Y_copied")
        s_Yt = sem("Y_transposed")
        s_y = sem("y_copied")
        s_y2 = sem("y_squared")
        s_yw = sem("gelu_argument")
        s_yt = sem("gelu_tanh")
        s_yg = sem("gelu_ready")
        s_xh = sem("operand_hi")
        s_xl = sem("operand_lo")
        s_sq = sem("square_ready")
        s_st = sem("sum_of_squares_done")
        s_dg = sem("diagonal_ready")
        s_rb = sem("rstd_broadcast")
        s_xn = sem("x_normed")
        s_ph = sem("p_hi")
        s_pn = sem("p_transposed")
        s_r = sem("relu_ready")
        s_rq = sem("relu_squared")
        s_hl = sem("hidden_lo")
        s_ot = sem("output_transposed")
        s_oc = sem("output_copied")
        s_out = sem("output_stored")
        s_x1 = sem("residual_added")
        s_p = sem("p_loaded")
        s_dt = sem("step_sizes_ready")
        s_cx = sem("context_loaded")
        s_qkg = sem("head_gains_loaded")
        s_cxt = sem("context_transposed")
        s_cxc = sem("context_copied")
        s_lm = sem("lambda_sums_ready")
        s_le = sem("lambda_exponentials_ready")
        s_zf = sem("fourier_input_copied")
        s_d1 = sem("dft_multiplied")
        s_d1c = sem("dft_copied")
        s_d2 = sem("dft_of_groups_multiplied")
        s_brh = sem("branch_hi")
        s_brl = sem("branch_lo")
        s_cm = sem("conv_sums_multiplied")
        s_cy = sem("conv_ready")
        s_cc = sem("conv_centred")
        s_cz = sem("conv_normed")
        s_ct = sem("conv_tanh")
        s_cs = sem("conv_silu")
        s_qc = sem("head_block_copied")
        s_qn = sem("heads_ready")
        s_qt = sem("heads_transposed")
        s_qtc = sem("heads_transposed_copied")
        s_sm = sem("scores_multiplied")
        s_nm = sem("row_max_ready")
        s_ex = sem("exponentials_ready")
        s_wd = sem("differences_ready")
        s_tr = sem("probabilities_transposed")
        s_tc = sem("probabilities_copied")
        s_om = sem("head_output_multiplied")
        s_on = sem("head_output_normed")
        s_qv = sem("values_ready")
        s_oh = sem("heads_output_complete")
        s_ott = sem("heads_output_transposed")
        s_mx = sem("mixed_complete")
        s_mh = sem("mixed_hi")
        s_ml = sem("mixed_lo")
        s_ft = sem("ffn_tanh")
        s_fp = sem("ffn_product")
        s_fh = sem("ffn_hi")
        s_fl = sem("ffn_lo")
        s_cnat = sem("c_loaded")
        s_xnat = sem("x_loaded")
        s_vz = sem("vectors_cleared")
        s_ldt = sem("log_dt_spread")
        s_Bb = sem("b_scaled")
        s_mod = sem("modulation_ready")
        s_res = sem("residual_complete")
        s_squ = sem("square_summed")
        s_pl = sem("p_lo")

        def cols(w2d, c0):
            return w2d.rearrange("(k p) n -> p k n", p=P)[:, :, bass.ds(c0, 256)]

        glu = A["ssm_w_glu"][0]
        m1, m2 = A["mlp_w1"][0], A["mlp_w2"][0]
        plw, plg = A["ple_w"][0], A["ple_gate_w"][0]
        wada = A["w_ada_2"]

        phases = []

        def phase(*a, **k):
            phases.append(Phase(*a, **k))
            return phases[-1]

        ada = [phase(f"ada{l}", 24, 4, lambda it, j, l=l: cols(wada[l], it * 1024 + j * 256), [KD] * 4, 256)
               for l in range(LAYERS)]
        p_glu = phase("glu", 8, 4, lambda it, j: cols(glu, it * 512 + (j // 2) * 256 + (0 if j % 2 else D)),
                      [KD] * 4, 256)
        p_m1 = phase("mlp1", 16, 4, lambda it, j: cols(m1, it * 1024 + j * 256), [KD] * 4, 256)
        m2v = m2.rearrange("(b k p) n -> p b k n", b=4, p=P)
        p_m2 = phase("mlp2", 16, 8,
                     lambda it, j: m2v[:, j % 4, :, bass.ds(it * 512 + (j // 4) * 256, 256)],
                     [KD] * 8, 256, units=4)
        p_pl = phase("ple", 8, 4, lambda it, j: cols(plw if j % 2 else plg, it * 512 + (j // 2) * 256),
                     [KD, 2, KD, 2], 256)
        L2 = []
        for l in range(LAYERS):
            win, wf = A["w_in_2"][l], [A[n][l] for n in ("w_four_2", "w_conv_2", "w_gqa_2", "w_diff_2")]
            f1, f3, f2, wo = A["w_ffn1_2"][l], A["w_ffn3_2"][l], A["w_ffn2_2"][l], A["w_out_2"][l]
            f2v = f2.rearrange("(k p) n -> p k n", p=P)
            q = {}

            def heads(name, n, c0, l=l, win=win, q=q):
                q[name] = phase(f"{name}{l}", n, n, lambda it, j: cols(win, c0 + j * 256), [KD] * n, 256)

            def branch(b, l=l, win=win, wf=wf, q=q):
                q["b", b] = phase(f"branch{b}{l}", 8, 4,
                                  lambda it, j: cols(wf[b], it * 512 + (j // 2) * 256) if j % 2 else
                                  cols(win, it * 512 + (COL["gate"] + b * D + (j // 2) * 256)),
                                  [KD, 4] * 2, 256)

            q["cv"] = phase(f"conv{l}", 4, 4,
                            lambda it, j, win=win: cols(win, COL["conv"] + (0 if j % 2 else BW) + (j // 2) * 256),
                            [KD] * 4, 256)
            heads("zf", 2, COL["four"])
            branch(0)
            heads("gq", 2, COL["gq"])
            heads("gkv", 1, COL["gkv"])
            branch(1)
            heads("dq", 2, COL["dq"])
            heads("dk", 2, COL["dk"])
            branch(2)
            heads("dv", 2, COL["dv"])
            branch(3)
            q["wo"] = phase(f"out{l}", 4, 4, lambda it, j, wo=wo: cols(wo, it * 1024 + j * 256), [KD] * 4, 256)
            for half, (t0, nt, ns) in enumerate(((0, 12, (12,)), (12, 10, (8, 2)))):
                c0 = t0 * P
                for i, n in enumerate(ns):
                    q["f1", half, i] = phase(
                        f"ffn1_{l}{half}{i}", n, min(4, n),
                        lambda it, j, c0=c0, f1=f1, f3=f3: cols(f3 if j % 2 else f1, it * 512 + (c0 + (j // 2) * 256)),
                        [KD] * min(4, n), 256)
                    c0 += n * P
                q["f2", half] = phase(
                    f"ffn2_{l}{half}", 8, 4,
                    lambda it, j, t0=t0, nt=nt, f2v=f2v: f2v[:, t0:t0 + nt, bass.ds(it * 512 + j * P, P)],
                    [nt] * 4, P)
            L2.append(q)
        g0 = 0
        for p in phases:
            p.g0 = g0
            g0 += p.n
        ADA = p_glu.g0
        u0 = 0
        for p in phases[2:]:
            p.m0 = p.g0 - ADA
            p.u0 = u0
            u0 += p.n // p.units
        NBLK = g0
        kt_of = {}
        for p in phases:
            for i in range(p.n):
                kt_of[p.g0 + i] = p.kts[i % p.body]

        def rawv(slot, kt, ncol=256):
            return raw[:, slot, 0:kt * ncol].rearrange("p (k n) -> p k n", k=kt)

        def half_shape(p, j):
            return (p.kts[j], P) if p.cols == 256 else (p.kts[j] // 2, p.cols)

        def raw_half(p, j, h):
            kt, n = half_shape(p, j)
            r = rawv((p.g0 + j) % RING, p.kts[j], p.cols)
            return r[:, :, h * P:h * P + P] if p.cols == 256 else r[:, h * kt:(h + 1) * kt, :]

        def split_half(t, p, j, h):
            kt, n = half_shape(p, j)
            o = h * (SLOT // 2)
            return t[:, (p.m0 + j) % 2, o:o + kt * n].rearrange("p (k n) -> p k n", k=kt)

        NAT_SP = 5 + 2 + 9 + 3

        def load(sp, p, it):
            for j in range(p.body):
                g = p.g0 + j
                first = g + (it if isinstance(it, int) else 1) * p.body
                if first >= ADA + RING:
                    sp.wait_ge(w_ready, it * (2 * p.body) + 2 * (g - RING - ADA + 1))
                elif first >= RING:
                    sp.wait_ge(ada_used, it * p.body + (g - RING + 1))
                sp.dma_start(rawv(g % RING, p.kts[j], p.cols), p.src(it, j)).then_inc(landed[g % RING], 16)

        def has_landed(eng, p, it, j):
            g = p.g0 + j
            if p.n > p.body:
                assert p.body % RING == 0
                eng.wait_ge(landed[g % RING], it * (p.body // RING * 16) + (g // RING + 1) * 16)
            else:
                eng.wait_ge(landed[g % RING], 16 * (g // RING + 1))

        block = ctx.enter_context(nc.Block())

        @block.sync
        def _(sp):
            sp.dma_start(const[:, :], A["consts"]).then_inc(s_const, 16)
            vec = [(0, "b_ada_2", 96), (96, "norm_mix", 8), (104, "norm_ffn", 8), (112, "norm_ple", 8),
                   (120, "norm_final", 8)]
            vec3 = [("norm_mix_2", 16), ("norm_ffn_2", 16), ("final_norm_2", 8), ("conv_b_2", 8),
                    ("conv_ln_g_2", 8), ("conv_ln_b_2", 8), ("c_2", 8), ("c_ctx_2", 8), ("diff_norm_2", 2)]

            def rows(name):
                a = A[name]
                if len(a.shape) == 2:
                    a = a.rearrange("l n -> (l n)")
                return a.rearrange("(r p) -> r p", p=P)

            sp.wait_ge(s_vz, 1)
            nd = 0
            for r, n, k in vec:
                sp.dma_start(vnat[r:r + k, 0, :], rows(n)).then_inc(s_nat, 16)
                nd += 1
            for l in range(LAYERS):
                sp.dma_start(vnat[0:TAPS * 4, 1 + l, :],
                             A["conv_w_2"][l].rearrange("k (t p) -> (k t) p", p=P)).then_inc(s_nat, 16)
                nd += 1
            r = 0
            for n, k in vec3:
                sp.dma_start(vnat[r:r + k, 3, :], rows(n)).then_inc(s_nat, 16)
                r += k
                nd += 1
            sp.dma_start(lnat[:, 0, :], A["ssm_lam_re"][0].rearrange("(q g) p -> q (g p)", g=2)).then_inc(s_nat, 16)
            sp.dma_start(lnat[:, 1, :], A["ssm_lam_im"][0].rearrange("(q g) p -> q (g p)", g=2)).then_inc(s_nat, 16)
            sp.dma_start(lnat[:, 3, 0:2], A["ssm_log_dt"][0].rearrange("(q g) -> q g", g=2)).then_inc(s_nat, 16)
            nd += 3
            assert nd == NAT_SP
            for p in phases:
                if p.n // p.body >= 4:
                    repeat(sp, p.n // p.body, lambda it, p=p: load(sp, p, it), peel_first=(p is ada[0]))
                else:
                    for it in range(p.n // p.body):
                        load(sp, p, it)
            sp.wait_ge(s_out, 16 * 2)


        def first(it):
            return it if isinstance(it, int) else 1

        def unit_view(p, j, T):
            return gb[:, 2 * unit(p, j)[0], 0:T]

        def tview(p, j, nt):
            b = 2 * unit(p, j)[0]
            return gb[:, b:b + 2, :].rearrange("p b (t n) -> p (b t) n", n=256)[:, 0:nt, :]

        def unit(p, j):
            u = p.u0 + j // p.units
            return u % 2, u // 2, p.body // p.units // 2

        def wait_drained(eng, p, it, j, more=0):
            b, n, per = unit(p, j)
            if n + more + it_min(it) * per > 0:
                eng.wait_ge(drained[b], it * per + (n + more))

        def it_min(it):
            return it if isinstance(it, int) else 0

        def multiplied(eng, p, it, j):
            eng.wait_ge(mm_done, it * (2 * p.body) + 2 * (p.m0 + j + 1))

        def gview(p, j, T):
            b = 2 * unit(p, j)[0]
            if T == 256 and p.units == 1:
                return gb[:, b, :].rearrange("p (b t) -> p b t", b=2)
            return gb[:, b:b + 2, 0:T]

        def two(t, slot, T):
            return t[:, slot, 0:2 * T].rearrange("p (b t) -> p b t", b=2)

        def split_hi(act, g, h):
            p, it, j = g
            m = p.m0 + j
            has_landed(act, p, it, j)
            if m + first(it) * p.body >= 2:
                act.wait_ge(mm_done, it * (2 * p.body) + (2 * (m - 2) + h + 1))
            nc.scalar.copy(split_half(wh, p, j, h), raw_half(p, j, h)).then_inc(hi_ready, 1)

        def ahead(p, it, j):
            if j + 2 < p.body:
                return (p, it, j + 2)
            if not isinstance(it, int) or it < p.n // p.body - 1:
                return (p, it + 1, j + 2 - p.body)
            k, rest = phases.index(p) + 1, j + 2 - p.body
            while k < len(phases) and rest >= phases[k].n:
                rest -= phases[k].n
                k += 1
            return None if k == len(phases) else (phases[k], rest // phases[k].body, rest % phases[k].body)

        def gemm_act(act, p, evac, before=None):
            def turn(it):
                for j in range(p.body):
                    if before is not None:
                        before(it, j)
                    nxt = ahead(p, it, j)
                    if nxt is not None:
                        split_hi(act, nxt, 0)
                    evac(it, j)
                    if nxt is not None:
                        split_hi(act, nxt, 1)
            repeat(act, p.n // p.body, turn, peel_last=True)

        def pair_tanh(act, p, T, th=th):
            def evac(it, j):
                if j % 2 == 0:
                    multiplied(act, p, it, j)
                    nc.scalar.activation(two(th, (j // 2) % 2, T), gview(p, j, T), ACT.Tanh, scale=0.5)\
                        .then_inc(drained[unit(p, j)[0]], 1)
            return evac

        NORMS = [(KD, SEQ, True), (KD, SEQ, True), (KD, SEQ, False)]
        for l in range(LAYERS):
            T = SEQ + CTX if l == 0 else SEQ
            NORMS += [(KD, SEQ + CTX, True), (4, T, False), (KD, T, True)]
        NORMS += [(KD, SEQ, False)]
        sq0 = [sum(m[0] for m in NORMS[:n]) for n in range(len(NORMS) + 1)]
        op0 = [KD + KD * sum(m[2] for m in NORMS[:n]) for n in range(len(NORMS) + 1)]

        def norm_act(act, n, src, ring, ready=None):
            kt, T, _ = NORMS[n]
            for k in range(kt):
                if ready is not None:
                    ready(k)
                if sq0[n] + k >= 4:
                    act.wait_ge(s_squ, sq0[n] + k - 3)
                nc.scalar.activation(ring[:, k % 4, 0:T], src(k), ACT.Square).then_inc(s_sq, 1)

        def norm_pe(pe, n, ring, dg):
            kt, T, _ = NORMS[n]
            for k in range(kt):
                pe.wait_ge(s_sq, sq0[n] + k + 1)
                for t in range(T // P):
                    ins = nc.tensor.matmul(mb[:, t, 0:1], ring[:, k % 4, t * P:t * P + P], ones[:, 0:1],
                                           start=(k == 0), stop=(k == kt - 1))
                ins.then_inc(s_squ, 1)
            pe.wait_ge(s_dg, n + 1)
            for t in range(T // P):
                ins = nc.tensor.matmul(mb[:, 0, t * P:t * P + P], ones[:, :], dg[:, t, :], start=True, stop=True)
            ins.then_inc(s_rb, 1)

        def rsqrt(T1, ms, y, t, ib, total, scale, eps):
            def step(ins):
                T1.add(ins)
                T1.wait()
            v = nc.vector
            step(v.tensor_scalar(ms, total, scale, eps, ALU.mult, ALU.add))
            step(v.tensor_scalar(ib.bitcast(I32), ms.bitcast(I32), 1, None, ALU.arith_shift_right))
            step(v.tensor_scalar(y.bitcast(I32), ib.bitcast(I32), -1.0, 1597463007.0, ALU.mult, ALU.add))
            for _ in range(3):
                step(v.tensor_tensor(t, y, y, ALU.mult))
                step(v.scalar_tensor_tensor(t, t, -0.5, ms, ALU.mult, ALU.mult))
                step(v.scalar_tensor_tensor(y, t, 1.5, y, ALU.add, ALU.mult))

        def rms_dve(dve, T1, n, dg, count, eps):
            kt, T, _ = NORMS[n]
            nt = T // P
            dve.wait_ge(s_squ, sq0[n + 1])
            rsqrt(T1, rs[:, 0, 0:nt], rs[:, 1, 0:nt], rs[:, 2, 0:nt], rs[:, 3, 0:nt],
                  mb[:, 0:nt, 0:1].rearrange("p a b -> p (a b)"), 1.0 / count, eps)
            for t in range(nt):
                T1.add(nc.vector.tensor_scalar(dg[:, t, :], ident, rs[:, 1, t:t + 1], None, ALU.mult))
            T1.wait()
            dve.sem_inc(s_dg, 1)
            dve.wait_ge(s_rb, n + 1)

        def parts(T):
            return [slice(0, SEQ)] if T == SEQ else [slice(0, SEQ), slice(SEQ, SEQ + CTX)]

        def operand_act(act, n, ring, shift=None):
            _, T, _ = NORMS[n]
            for k in range(KD):
                act.wait_ge(s_xn, op0[n] - KD + k + 1)
                if shift is None:
                    nc.scalar.copy(xh[:, k, 0:T], ring[:, k % 4, 0:T]).then_inc(s_xh, 1)
                else:
                    for i, part in enumerate(parts(T)):
                        ins = nc.scalar.activation(xh[:, k, part], ring[:, k % 4, part], ACT.Identity,
                                                   bias=shift(k, i))
                    ins.then_inc(s_xh, 1)

        def norm_dve(dve, T1, n, gain, ring, dg, in_place=False, shift=None):
            _, T, _ = NORMS[n]
            rms_dve(dve, T1, n, dg, D, EPS)
            if in_place:
                for k in range(KD):
                    T1.add(nc.vector.scalar_tensor_tensor(x[:, k, 0:T], x[:, k, 0:T], gain(k, 0),
                                                          mb[:, 0, 0:T], ALU.mult, ALU.mult))
                T1.wait()
                return
            for k in range(KD + 1):
                if k < KD:
                    for i, part in enumerate(parts(T)):
                        ins = nc.vector.scalar_tensor_tensor(ring[:, k % 4, part], x[:, k, part], gain(k, i),
                                                             mb[:, 0, part], ALU.mult, ALU.mult)
                        if i < len(parts(T)) - 1:
                            T1.add(ins)
                    ins.then_inc(s_xn, 1)
                if k:
                    dve.wait_ge(s_xh, op0[n] + k)
                    for i, part in enumerate(parts(T)):
                        src, hi = ring[:, (k - 1) % 4, part], xh[:, k - 1, part].bitcast(F32)
                        if shift is None:
                            ins = nc.vector.tensor_tensor(xl[:, k - 1, part], src, hi, ALU.subtract)
                        else:
                            ins = nc.vector.scalar_tensor_tensor(xl[:, k - 1, part], src, shift(k - 1, i), hi,
                                                                 ALU.add, ALU.subtract)
                        if i < len(parts(T)) - 1:
                            T1.add(ins)
                    ins.then_inc(s_xl, 1)

        def vec(col):
            return lambda k, i: vecs[:, col + k:col + k + 1]

        def yview(d):
            return gb[:, 2 + d % 2, 0:256]

        RES_END = 9
        ITEMS = []
        nsc = 0
        for l in range(LAYERS):
            for kind, nh in (("g", 8), ("d", 4)):
                for t in range(4 if l == 0 else 2):
                    keys = (0, SEQ + CTX) if t < 2 else (SEQ, SEQ + CTX)
                    for h in range(nh):
                        ITEMS.append((l, kind, t, h, keys, nsc))
                        nsc += 1 if kind == "g" else 2

        def items(l, kind):
            return [n for n, it in enumerate(ITEMS) if it[0] == l and it[1] == kind]

        def scores_of(n):
            return range(ITEMS[n][5], ITEMS[n][5] + (1 if ITEMS[n][1] == "g" else 2))

        item_of = {c: n for n in range(len(ITEMS)) for c in scores_of(n)}

        def nk(n):
            return ITEMS[n][4][1] - ITEMS[n][4][0]

        def attend_pe(pe, l, kind):
            mine = items(l, kind)
            pe.wait_ge(s_qtc, TN[l, kind] + len(tlist(l, kind)))

            def scores(n):
                _, _, t, h, (k0, k1), c0 = ITEMS[n]
                for c in scores_of(n):
                    if c >= 4:
                        pe.wait_ge(s_ex, c - 3)
                    if kind == "g":
                        r, tile = slice(64 * (h % 2), 64 * (h % 2) + 64), h // 2
                        lhs, rhs = gqT[r, tile, t * P:t * P + P], gkT[r, k0:k1]
                    else:
                        r = slice(64 * (c - c0), 64 * (c - c0) + 64)
                        lhs, rhs = dqT[r, h, t * P:t * P + P], dkT[r, h, k0:k1]
                    nc.tensor.matmul(gb[:, c % 4, 0:k1 - k0], lhs, rhs, start=True, stop=True).then_inc(s_sm, 1)

            def transposes(n):
                if kind == "g":
                    pe.wait_ge(s_ex, ITEMS[n][5] + 1)
                else:
                    pe.wait_ge(s_wd, diff_index(n) + 1)
                if n >= 2:
                    pe.wait_ge(s_tc, n - 1)
                for k in range(nk(n) // P):
                    ins = nc.tensor.transpose(mb[:, n % 2, k * P:k * P + P],
                                              probs[:, ITEMS[n][5] % PROBS, k * P:k * P + P], ident)
                ins.then_inc(s_tr, 1)

            def outputs(n):
                _, _, t, h, (k0, k1), c0 = ITEMS[n]
                pe.wait_ge(s_tc, n + 1)
                if n >= 2:
                    pe.wait_ge(s_on, n - 1)
                for k in range(nk(n) // P):
                    kt = k0 // P + k
                    if kind == "g":
                        rhs, w = gkv[:, kt, P + 64 * (h % 2):P + 64 * (h % 2) + 64], 64
                    else:
                        rhs, w = dk[:, kt, h * P:h * P + P], P
                    ins = nc.tensor.matmul(mb[:, 2 + n % 2, 0:w], probt[:, n % 2, k * P:k * P + P], rhs,
                                           start=(k == 0), stop=(k == nk(n) // P - 1))
                ins.then_inc(s_om, 1)

            for i in range(len(mine) + 3):
                if i < len(mine):
                    scores(mine[i])
                if 2 <= i < len(mine) + 2:
                    transposes(mine[i - 2])
                if i >= 3:
                    outputs(mine[i - 3])

        def diff_index(n):
            return sum(ITEMS[m][1] == "d" for m in range(n))

        def attend_act(act, l, kind):
            mine = items(l, kind)

            def exps(n):
                for c in scores_of(n):
                    act.wait_ge(s_nm, c + 1)
                    if c >= PROBS:
                        act.wait_ge(s_tr, item_of[c - PROBS] + 1)
                    if c >= 8:
                        act.wait_ge(s_on, item_of[c - 8] + 1)
                    nc.scalar.activation(probs[:, c % PROBS, 0:nk(n)], gb[:, c % 4, 0:nk(n)], ACT.Exp,
                                         bias=mx[:, 0, c % 8:c % 8 + 1], scale=1.0,
                                         accum_out=mx[:, 1, c % 8:c % 8 + 1]).then_inc(s_ex, 1)

            def copies(n):
                act.wait_ge(s_tr, n + 1)
                if n >= 2:
                    act.wait_ge(s_om, n - 1)
                nc.scalar.copy(probt[:, n % 2, 0:nk(n)], mb[:, n % 2, 0:nk(n)]).then_inc(s_tc, 1)

            for i in range(len(mine) + 2):
                if i < len(mine):
                    exps(mine[i])
                if i >= 2:
                    copies(mine[i - 2])

        def attend_dve(dve, D1, l, kind, o):
            mine = items(l, kind)
            v = nc.vector

            def maxima(n):
                for c in scores_of(n):
                    dve.wait_ge(s_sm, c + 1)
                    if c >= 8:
                        dve.wait_ge(s_ex, c - 7)
                    v.tensor_reduce(mx[:, 0, c % 8:c % 8 + 1], gb[:, c % 4, 0:nk(n)], AX_X, ALU.max, negate=True)\
                        .then_inc(s_nm, 1)

            def difference(n):
                c = ITEMS[n][5]
                dve.wait_ge(s_ex, c + 2)
                D1.add(v.reciprocal(mx[:, 2, c % 8:c % 8 + 2], mx[:, 1, c % 8:c % 8 + 2]))
                D1.wait()
                D1.add(v.tensor_scalar(mx[:, 2, (c + 1) % 8:(c + 1) % 8 + 1], mx[:, 2, (c + 1) % 8:(c + 1) % 8 + 1],
                                       lamb[:, l:l + 1], None, ALU.mult))
                D1.wait()
                p0, p1 = probs[:, c % PROBS, 0:nk(n)], probs[:, (c + 1) % PROBS, 0:nk(n)]
                D1.add(v.tensor_scalar(p1, p1, mx[:, 2, (c + 1) % 8:(c + 1) % 8 + 1], None, ALU.mult))
                D1.wait()
                v.scalar_tensor_tensor(p0, p0, mx[:, 2, c % 8:c % 8 + 1], p1, ALU.mult, ALU.add).then_inc(s_wd, 1)

            def outs(n):
                _, _, t, h, _, c = ITEMS[n]
                if kind == "g":
                    D1.add(v.reciprocal(mx[:, 2, c % 8:c % 8 + 1], mx[:, 1, c % 8:c % 8 + 1]))
                    D1.wait()
                    head = h // 2 + 4 * (h % 2)
                    dve.wait_ge(s_om, n + 1)
                    v.tensor_scalar(o[:, t, head * 64:head * 64 + 64], mb[:, 2 + n % 2, 0:64],
                                    mx[:, 2, c % 8:c % 8 + 1], None, ALU.mult).then_inc(s_on, 1)
                else:
                    dve.wait_ge(s_om, n + 1)
                    v.tensor_copy(o[:, t, h * P:h * P + P], mb[:, 2 + n % 2, 0:P]).then_inc(s_on, 1)

            for i in range(len(mine) + 3):
                if i < len(mine):
                    maxima(mine[i])
                if 1 <= i <= len(mine) and kind == "d":
                    difference(mine[i - 1])
                if i >= 3:
                    outs(mine[i - 3])

        BR = [0]

        def br_index(l, b):
            return l * 4 + b

        def branch_ready(pe, l, b):
            def need(it, j, k):
                if isinstance(it, int) and it == 0 and j == 1:
                    pe.wait_ge(s_brl, 4 * br_index(l, b) + k + 1)
            return need

        HB = {"zf": 0, "gq": 2, "gkv": 4, "dq": 5, "dk": 7, "dv": 9}
        HBL = 11

        def heads_act(act, l, name, nt):
            p = L2[l][name]

            def evac(it, j):
                multiplied(act, p, it, j)
                src = tview(p, j, nt)
                if name == "gq":
                    dst = gq[:, 0:nt, :].rearrange("p t (i e d) -> p t i e d", i=4, e=2)[:, :, :, j, :]
                    src = src.rearrange("p t (i d) -> p t i d", i=4)
                else:
                    buf = {"zf": zf, "gkv": gkv, "dq": dq, "dk": dk, "dv": dk}[name]
                    dst = buf[:, 0:nt, j * 256:(j + 1) * 256]
                if name == "gq":
                    for t in range(nt):
                        ins = nc.scalar.copy(dst[:, t], src[:, t])
                        if t < nt - 1:
                            ins.then_inc(s_act, 1)
                            ACT_N[0] += 1
                else:
                    ins = nc.scalar.copy(dst, src)
                ins.then_inc(drained[unit(p, j)[0]], 1)
            gemm_act(act, p, evac)

        ACT_N = [0]

        def heads_pe(pe, l, name, nt, need=None):
            p = L2[l][name]
            for j in range(p.n):
                m = p.m0 + j
                wait_drained(pe, p, 0, j)
                pe.wait_ge(w_ready, 2 * m + 2)
                g = tview(p, j, nt)
                H = wh[:, m % 2, :].rearrange("p (h k n) -> p k h n", h=2, k=KD)
                L = wl[:, m % 2, :].rearrange("p (h k n) -> p k h n", h=2, k=KD)
                for t in range(nt):
                    ts = slice(t * P, t * P + P)
                    for k in range(KD):
                        nc.tensor.matmul(g[:, t, :], xh[:, k, ts], H[:, k], start=(k == 0), stop=False)
                        nc.tensor.matmul(g[:, t, :], xl[:, k, ts], H[:, k], start=False, stop=False)
                        ins = nc.tensor.matmul(g[:, t, :], xh[:, k, ts], L[:, k], start=False, stop=(k == KD - 1))
                ins.then_inc(mm_done, 2)

        def all_drained(eng, p):
            u = p.u0 + p.n // p.units
            for b in range(2):
                n = (u + 1 - b) // 2
                if n:
                    eng.wait_ge(drained[b], n)

        def layer_T(l):
            return SEQ + CTX if l == 0 else SEQ

        def X2(T):
            return lambda j, k: (xh[:, k, 0:T], xl[:, k, 0:T])

        def XB(T):
            return lambda j, k: (brh[:, k, 0:T], brl[:, k, 0:T]) if j % 2 else (xh[:, k, 0:T], xl[:, k, 0:T])

        def shift_of(l, c):
            return lambda k, i: mod[:, l, c + k, i:i + 1]

        def gain_of(l, c):
            return lambda k, i: msc[:, l, c, k, i:i + 1]

        def layer_pe(pe, l):
            q, T = L2[l], layer_T(l)
            nt = T // P
            n0 = 3 + 3 * l
            norm_pe(pe, n0, sqr2, dg2)
            gemm_pe(pe, q["cv"], T, X2(T), first_use(pe, s_xl, op0[n0]))
            heads_pe(pe, l, "zf", nt)
            for s_ in range(nt // 2):
                i = s_ + 2 * l
                if s_ == 0:
                    all_drained(pe, q["zf"])
                if i:
                    pe.wait_ge(s_brh, 4 * br_index(l, 0) + 4 * s_) if s_ else None
                    pe.wait_ge(s_brl, 4 * br_index(l, 0) + 4 * s_) if s_ else None
                for f in range(4):
                    for k in range(2):
                        ins = nc.tensor.matmul(mb[:, f, :], zf[:, 2 * s_ + k, f * P:f * P + P],
                                               const[:, C_DFT + 512 * k:C_DFT + 512 * k + 512],
                                               start=(k == 0), stop=(k == 1))
                ins.then_inc(s_d1, 1)
                pe.wait_ge(s_d1c, i + 1)
                for f in range(4):
                    for k in range(2):
                        ins = nc.tensor.matmul(mb[:, f, 0:SEQ], const[:, C_DIM + P * k:C_DIM + P * k + P],
                                               dft1[:, f, SEQ * k:SEQ * k + SEQ], start=(k == 0), stop=(k == 1))
                ins.then_inc(s_d2, 1)
            gemm_pe(pe, q["b", 0], T, XB(T), branch4(pe, l, 0))
            heads_pe(pe, l, "gq", nt)
            heads_pe(pe, l, "gkv", 4)
            pe.wait_ge(s_cy, l + 1)
            pe.wait_ge(s_brl, 4 * DFTB[l])
            for f in range(4):
                ins = nc.tensor.matmul(mb[:, 1, 0:T], ones[:, :], cy[:, f, 0:T], start=(f == 0), stop=(f == 3))
            ins.then_inc(s_cm, 1)
            pe.wait_ge(s_cc, 4 * l + 4)
            norm_pe_ln(pe, n0 + 1)
            gemm_pe(pe, q["b", 1], T, XB(T), branch4(pe, l, 1))
            transposes_pe(pe, l, "g")
            attend_pe(pe, l, "g")
            back_pe(pe, l, "g", gq)
            heads_pe(pe, l, "dq", nt)
            heads_pe(pe, l, "dk", 4)
            gemm_pe(pe, q["b", 2], T, XB(T), branch4(pe, l, 2))
            transposes_pe(pe, l, "d")
            heads_pe(pe, l, "dv", 4)
            pe.wait_ge(s_qv, l + 1)
            attend_pe(pe, l, "d")
            gemm_pe(pe, q["b", 3], T, XB(T), branch4(pe, l, 3, lambda: back_pe(pe, l, "d", dq)))
            gemm_pe(pe, q["wo"], T, X2(T), first_use(pe, s_ml, 8 * l))
            norm_pe(pe, n0 + 2, sqr2, dg2)
            for half in range(2):
                for i in range(1 + half):
                    gemm_pe(pe, q["f1", half, i], T, X2(T), None if half else first_use(pe, s_xl, op0[n0 + 2]))
                pe.wait_ge(s_fl, FL[l][half])
                ffn2_pe(pe, q["f2", half], T)

        def first_use(pe, sem_, n):
            def need(it, j, k):
                if isinstance(it, int) and it == 0 and j == 0:
                    pe.wait_ge(sem_, n + k + 1)
            return need

        def branch4(pe, l, b, before=None):
            def need(it, j, k):
                if isinstance(it, int) and it == 0 and j == 1 and k == 0:
                    if before is not None:
                        before()
                    pe.wait_ge(s_brl, 4 * BRN[l][b])
            return need

        BRN, n_ = [], 0
        for l in range(LAYERS):
            row = []
            for b in range(4):
                n_ += (layer_T(l) // SEQ if b == 0 else 1)
                row.append(n_)
            BRN.append(row)
        DFTB = [BRN[l][0] for l in range(LAYERS)]
        FL = [[6, 11], [17, 22]]

        def norm_pe_ln(pe, n):
            norm_pe(pe, n, sqr2, dg2)

        def transposes_pe(pe, l, kind):
            nt = layer_T(l) // P
            pe.wait_ge(s_qn, 2 * l + (1 if kind == "g" else 2))
            todo = tlist(l, kind)
            for i, (src, dst, w, ntk) in enumerate(todo):
                n = TN[l, kind] + i
                if i >= 4:
                    pe.wait_ge(s_qtc, n - 3)
                for t in range(ntk):
                    ins = nc.tensor.transpose(mb[:, i % 4, t * P:t * P + P], src[:, t, w:w + P], ident)
                ins.then_inc(s_qt, 1)

        def tlist(l, kind):
            nt = layer_T(l) // P
            if kind == "g":
                return [(gq, gqT[:, f, :], f * P, nt) for f in range(4)] + [(gkv, gkT[:, :], 0, 4)]
            return [(dq, dqT[:, f, :], f * P, nt) for f in range(4)] + [(dk, dkT[:, f, :], f * P, 4) for f in range(4)]

        TN, n_ = {}, 0
        for l in range(LAYERS):
            for kind in "gd":
                TN[l, kind] = n_
                n_ += 5 if kind == "g" else 8

        def transposes_act(act, l, kind):
            for i, (src, dst, w, ntk) in enumerate(tlist(l, kind)):
                act.wait_ge(s_qt, TN[l, kind] + i + 1)
                scale = 0.125 if i < 4 else 1.0
                nc.scalar.activation(dst[:, 0:ntk * P], mb[:, i % 4, 0:ntk * P], ACT.Copy, scale=scale)\
                    .then_inc(s_qtc, 1)

        def back_pe(pe, l, kind, o):
            nt = layer_T(l) // P
            pe.wait_ge(s_oh, 2 * l + (1 if kind == "g" else 2))
            for f in range(4):
                for t in range(nt):
                    ins = nc.tensor.transpose(mb[:, f, t * P:t * P + P], o[:, t, f * P:f * P + P], ident)
            ins.then_inc(s_ott, 1)

        def ffn2_pe(pe, p, T):
            def turn(it):
                for j in range(p.body):
                    m, kt = p.m0 + j, p.kts[j]
                    wait_drained(pe, p, it, j)
                    o = unit_view(p, j, T)
                    for k in range(kt):
                        h, kk = divmod(k, kt // 2)
                        if kk == 0:
                            pe.wait_ge(w_ready, it * (2 * p.body) + (2 * m + h + 1))
                            H, L = split_half(wh, p, j, h), split_half(wl, p, j, h)
                        XH, XL = fhh[:, k, 0:T], fhl[:, k, 0:T]
                        nc.tensor.matmul(o, H[:, kk, :], XH, start=(k == 0), stop=False)
                        nc.tensor.matmul(o, H[:, kk, :], XL, start=False, stop=False)
                        ins = nc.tensor.matmul(o, L[:, kk, :], XH, start=False, stop=(k == kt - 1))
                        if kk == kt // 2 - 1:
                            ins.then_inc(mm_done, 1)
            repeat(pe, p.n // p.body, turn)

        def layer_act(act, l):
            q, T = L2[l], layer_T(l)
            nt = T // P
            n0 = 3 + 3 * l
            norm_act(act, n0, lambda k: x[:, k, :], sqr2)
            operand_act(act, n0, sqr2, shift_of(l, 0))
            gemm_act(act, q["cv"], pair_tanh(act, q["cv"], T, th2))
            heads_act(act, l, "zf", nt)
            for s_ in range(nt // 2):
                i = s_ + 2 * l
                act.wait_ge(s_d1, i + 1)
                nc.scalar.copy(dft1[:, :, :], mb[:, :, :]).then_inc(s_d1c, 1)
                act.wait_ge(s_d2, i + 1)
                if s_ == 0 and l:
                    act.wait_ge(mm_done, 2 * q["zf"].m0)
                for f in range(4):
                    nc.scalar.copy(brh[:, f, s_ * SEQ:(s_ + 1) * SEQ], mb[:, f, 0:SEQ]).then_inc(s_brh, 1)
            gemm_act(act, q["b", 0], pair_tanh(act, q["b", 0], T, th2))
            heads_act(act, l, "gq", nt)
            heads_act(act, l, "gkv", 4)
            norm_act(act, n0 + 1, lambda k: cy[:, k, 0:T], sqr2,
                     ready=lambda k: act.wait_ge(s_cc, 4 * l + k + 1))
            act.wait_ge(mm_done, 2 * (q["b", 0].m0 + 8))
            for f in range(4):
                act.wait_ge(s_cz, 4 * l + f + 1)
                nc.scalar.activation(sqr2[:, f, 0:T], cy[:, f, 0:T], ACT.Tanh, scale=0.5).then_inc(s_ct, 1)
            for f in range(4):
                act.wait_ge(s_cs, 4 * l + f + 1)
                nc.scalar.copy(brh[:, f, 0:T], sqr2[:, f, 0:T]).then_inc(s_brh, 1)
            gemm_act(act, q["b", 1], pair_tanh(act, q["b", 1], T, th2))
            transposes_act(act, l, "g")
            attend_act(act, l, "g")
            back_act(act, l, 2)
            heads_act(act, l, "dq", nt)
            heads_act(act, l, "dk", 4)
            gemm_act(act, q["b", 2], pair_tanh(act, q["b", 2], T, th2))
            transposes_act(act, l, "d")
            heads_act(act, l, "dv", 4)
            attend_act(act, l, "d")
            gemm_act(act, q["b", 3], pair_tanh(act, q["b", 3], T, th2),
                     before=lambda it, j: back_act(act, l, 3) if (it, j) == (0, 1) else None)
            act.wait_ge(s_mx, l + 1)
            act.wait_ge(mm_done, 2 * q["wo"].m0)
            for k in range(KD):
                nc.scalar.copy(xh[:, k, 0:T], mix[:, k, 0:T]).then_inc(s_mh, 1)
            gemm_act(act, q["wo"], lambda it, j: None)
            act.wait_ge(s_res, 5 + 2 * l)
            norm_act(act, n0 + 2, lambda k: x[:, k, 0:T], sqr2)
            operand_act(act, n0 + 2, sqr2, shift_of(l, 24))
            for half in range(2):
                for i in range(1 + half):
                    ffn1_act(act, l, half, i, T)
                gemm_act(act, q["f2", half], lambda it, j: None)
            act.wait_ge(s_res, 6 + 2 * l)

        def ffn_pair0(l, half, i):
            return 11 * l + 6 * half + 4 * i

        def ffn1_act(act, l, half, i, T):
            p, n0 = L2[l]["f1", half, i], ffn_pair0(l, half, i)
            t0 = 4 * 2 * i if half else 0

            def evac(it, j):
                pair = it * 2 + j // 2
                if j % 2 == 0:
                    multiplied(act, p, it, j)
                    nc.scalar.activation(two(th2, (j // 2) % 2, T), gview(p, j, T), ACT.Tanh, scale=0.5)\
                        .then_inc(s_ft, 1)
                else:
                    if half and i == 0 and j == 1 and it == 0:
                        act.wait_ge(mm_done, 2 * (L2[l]["f2", 0].m0 + 8))
                    act.wait_ge(s_fp, it * 2 + (n0 + j // 2 + 1))
                    nc.scalar.copy(fhh[:, bass.ds(it * 4 + (t0 + 2 * (j // 2)), 2), 0:T], two(pr2, (j // 2) % 2, T))\
                        .then_inc(s_fh, 1)
            trips = p.n // p.body
            for it in range(trips):
                for j in range(p.body):
                    nxt = ahead(p, it, j)
                    if nxt is not None:
                        split_hi(act, nxt, 0)
                    evac(it, j)
                    if nxt is not None:
                        split_hi(act, nxt, 1)

        def back_act(act, l, b):
            T = layer_T(l)
            act.wait_ge(s_ott, 2 * l + b - 1)
            for f in range(4):
                src = mb[:, f, 0:T]
                if b == 3:
                    nc.scalar.activation(brh[:, f, 0:T], src, ACT.Copy, scale=dgain[:, l:l + 1]).then_inc(s_brh, 1)
                else:
                    nc.scalar.copy(brh[:, f, 0:T], src).then_inc(s_brh, 1)

        def layer_dve(dve, D1, l):
            q, T = L2[l], layer_T(l)
            nt, ns = T // P, T // SEQ
            n0 = 3 + 3 * l
            v = nc.vector

            def step(ins):
                D1.add(ins)
                D1.wait()

            norm_dve(dve, D1, n0, gain_of(l, 0), sqr2, dg2, shift=shift_of(l, 0))
            p = q["cv"]
            pad = (TAPS - 1) // 2
            D1.add(v.memset(upad[:, :, 0:ns, 0:pad], 0.0))
            D1.add(v.memset(upad[:, :, 0:ns, pad + SEQ:], 0.0))
            for pair in range(2):
                j = 2 * pair
                wait_drained(dve, p, 0, j, 1)
                step(v.tensor_scalar(two(pr2, pair, T), two(th2, pair, T), 0.5, 0.5, ALU.mult, ALU.add))
                multiplied(dve, p, 0, j + 1)
                for i in range(2):
                    ins = v.tensor_tensor(upad[:, 2 * pair + i, 0:ns, pad:pad + SEQ],
                                          two(pr2, pair, T)[:, i, :].rearrange("p (s t) -> p s t", s=ns),
                                          gview(p, j + 1, T)[:, i, :].rearrange("p (s t) -> p s t", s=ns), ALU.mult)
                    if i == 0:
                        D1.add(ins)
                ins.then_inc(drained[unit(p, j + 1)[0]], 1)
                wait_drained(dve, p, 0, j + 1, 1)
            D1.wait()

            def taps(k0, k1):
                for k in range(k0, k1):
                    for f in range(4):
                        u = upad[:, f, 0:ns, k:k + SEQ]
                        a = cy[:, f, 0:T].rearrange("p (s t) -> p s t", s=ns)
                        w = vecs[:, V_CONVW + P * l + 4 * k + f:V_CONVW + P * l + 4 * k + f + 1]
                        if k == 0:
                            b = V_CB + 4 * l + f
                            D1.add(v.tensor_scalar(a, u, w, vecs[:, b:b + 1], ALU.mult, ALU.add))
                        else:
                            dve.wait_ge(s_dve, D1.n - 3)
                            D1.add(v.scalar_tensor_tensor(a, u, w, a, ALU.mult, ALU.add))

            for s_ in range(ns):
                i = s_ + 2 * l
                n = (BRN[l][0] - ns + s_) * 4
                for f in range(4):
                    dve.wait_ge(s_brh, n + f + 1)
                    v.tensor_tensor(brl[:, f, s_ * SEQ:(s_ + 1) * SEQ], mb[:, f, 0:SEQ],
                                    brh[:, f, s_ * SEQ:(s_ + 1) * SEQ].bitcast(F32), ALU.subtract).then_inc(s_brl, 1)

            def branch_dve(b, between=None):
                p = q["b", b]
                for it in range(2):
                    for j in range(0, 4, 2):
                        s_, pair = (j // 2) % 2, 2 * it + j // 2
                        wait_drained(dve, p, it, j, 1)
                        step(v.tensor_scalar(two(pr2, s_, T), two(th2, s_, T), 0.5, 0.5, ALU.mult, ALU.add))
                        multiplied(dve, p, it, j + 1)
                        dst = mix[:, 2 * pair:2 * pair + 2, 0:T]
                        prod = dst if b == 0 else two(pr2, s_, T)
                        v.tensor_tensor(prod, two(pr2, s_, T), gview(p, j + 1, T), ALU.mult)\
                            .then_inc(drained[unit(p, j + 1)[0]], 1)
                        wait_drained(dve, p, it, j + 1, 1)
                        if b:
                            D1.add(v.tensor_tensor(dst, dst, prod, ALU.add))
                        if between is not None:
                            between(pair)

            branch_dve(0, lambda pair: taps(8 * pair, min(8 * pair + 8, TAPS)))
            D1.wait()
            dve.sem_inc(s_cy, 1)
            dve.wait_ge(s_cm, l + 1)
            for f in range(4):
                v.scalar_tensor_tensor(cy[:, f, 0:T], mb[:, 1, 0:T], -1.0 / BW, cy[:, f, 0:T], ALU.mult, ALU.add)\
                    .then_inc(s_cc, 1)
            rms_dve(dve, D1, n0 + 1, dg2, BW, LN_EPS)
            for f in range(4):
                c = 4 * l + f
                step(v.tensor_tensor(cy[:, f, 0:T], cy[:, f, 0:T], mb[:, 0, 0:T], ALU.mult))
                v.tensor_scalar(cy[:, f, 0:T], cy[:, f, 0:T], vecs[:, V_LG + c:V_LG + c + 1],
                                vecs[:, V_LB + c:V_LB + c + 1], ALU.mult, ALU.add).then_inc(s_cz, 1)
            for f in range(4):
                dve.wait_ge(s_ct, 4 * l + f + 1)
                step(v.tensor_scalar(sqr2[:, f, 0:T], sqr2[:, f, 0:T], 0.5, 0.5, ALU.mult, ALU.add))
                v.tensor_tensor(sqr2[:, f, 0:T], sqr2[:, f, 0:T], cy[:, f, 0:T], ALU.mult).then_inc(s_cs, 1)
                n = (BRN[l][1] - 1) * 4
                dve.wait_ge(s_cs, 4 * l + f + 1)
                dve.wait_ge(s_brh, n + f + 1)
                v.tensor_tensor(brl[:, f, 0:T], sqr2[:, f, 0:T], brh[:, f, 0:T].bitcast(F32), ALU.subtract)\
                    .then_inc(s_brl, 1)

            def head_norm(t_, w, ntk, gain):
                nh = w // 64
                for t in range(ntk):
                    a = t_[:, t, 0:w].rearrange("p (h d) -> p h d", d=64)
                    b = tmp2[:, t % 2, 0:w].rearrange("p (h d) -> p h d", d=64)
                    step(v.tensor_tensor(b, a, a, ALU.mult))
                    D1.add(v.tensor_reduce(st[:, 0, t * nh:t * nh + nh], b, AX_X, ALU.add))
                    yield
                D1.wait()
                n = ntk * nh
                rsqrt(D1, st[:, 1, 0:n], st[:, 2, 0:n], st[:, 3, 0:n], st[:, 0, 0:n], st[:, 0, 0:n], 1.0 / 64, EPS)
                for t in range(ntk):
                    a = t_[:, t, 0:w].rearrange("p (h d) -> p h d", d=64)
                    step(v.tensor_tensor(a, a, st[:, 2, t * nh:t * nh + nh].unsqueeze(2).to_broadcast([P, nh, 64]),
                                         ALU.mult))
                    D1.add(v.tensor_tensor(a, a, gain.unsqueeze(1).to_broadcast([P, nh, 64]), ALU.mult))
                    yield
                D1.wait()

            def rotate(t_, w):
                nh = w // 64
                for t in range(2):
                    cs = [const[:, C_ROPE + 64 * t + 32 * i:C_ROPE + 64 * t + 32 * i + 32] for i in range(2)]
                    a = t_[:, t, 0:w].rearrange("p (h e d) -> p h e d", e=2, d=32)
                    b = tmp2[:, t, 0:w].rearrange("p (h e d) -> p h e d", e=2, d=32)
                    sn = cs[1].unsqueeze(1).to_broadcast([P, nh, 32])
                    D1.add(v.tensor_tensor(b[:, :, 0, :], a[:, :, 1, :], sn, ALU.mult))
                    step(v.tensor_tensor(b[:, :, 1, :], a[:, :, 0, :], sn, ALU.mult))
                    af = t_[:, t, 0:w].rearrange("p (h d) -> p h d", d=32)
                    step(v.tensor_tensor(af, af, cs[0].unsqueeze(1).to_broadcast([P, 2 * nh, 32]), ALU.mult))
                    D1.add(v.tensor_tensor(a[:, :, 0, :], a[:, :, 0, :], b[:, :, 0, :], ALU.subtract))
                    D1.add(v.tensor_tensor(a[:, :, 1, :], a[:, :, 1, :], b[:, :, 1, :], ALU.add))
                    yield
                D1.wait()

            def meanwhile(b, steps, share):
                todo = iter(steps)
                branch_dve(b, lambda pair: [next(todo, None) for _ in range(share)])
                for _ in todo:
                    pass
                D1.wait()
                dve.sem_inc(s_qn, 1)

            def grouped_heads():
                all_drained(dve, q["gkv"])
                yield from head_norm(gq, BW, nt, qkg[:, l, 0, :])
                yield from rotate(gq, BW)
                yield from head_norm(gkv, P, 4, qkg[:, l, 1, :])
                yield from rotate(gkv, P)

            meanwhile(1, grouped_heads(), 5)
            dve.wait_ge(s_qtc, TN[l, "g"] + 5)
            attend_dve(dve, D1, l, "g", gq)
            dve.wait_ge(s_on, items(l, "g")[-1] + 1)
            dve.sem_inc(s_oh, 1)
            back_dve(dve, l, 2)

            def differential_heads():
                all_drained(dve, q["dk"])
                yield from rotate(dq, BW)
                yield from rotate(dk, BW)

            meanwhile(2, differential_heads(), 1)
            all_drained(dve, q["dv"])
            dve.sem_inc(s_qv, 1)
            dve.wait_ge(s_qtc, TN[l, "d"] + 8)
            attend_dve(dve, D1, l, "d", dq)
            dve.wait_ge(s_on, items(l, "d")[-1] + 1)
            for t in range(nt):
                a = dq[:, t, :].rearrange("p (h d) -> p h d", d=P)
                b = tmp2[:, t % 2, :].rearrange("p (h d) -> p h d", d=P)
                step(v.tensor_tensor(b, a, a, ALU.mult))
                D1.add(v.tensor_reduce(st[:, 0, 4 * t:4 * t + 4], b, AX_X, ALU.add))
            D1.wait()
            n = 4 * nt
            rsqrt(D1, st[:, 1, 0:n], st[:, 2, 0:n], st[:, 3, 0:n], st[:, 0, 0:n], st[:, 0, 0:n], 1.0 / P, EPS)
            for t in range(nt):
                a = dq[:, t, :].rearrange("p (h d) -> p h d", d=P)
                D1.add(v.tensor_tensor(a, a, st[:, 2, 4 * t:4 * t + 4].unsqueeze(2).to_broadcast([P, 4, P]), ALU.mult))
            D1.wait()
            dve.sem_inc(s_oh, 1)
            back_dve(dve, l, 3)
            branch_dve(3)
            D1.wait()
            dve.sem_inc(s_mx, 1)
            for k in range(KD):
                dve.wait_ge(s_mh, 8 * l + k + 1)
                v.tensor_tensor(xl[:, k, 0:T], mix[:, k, 0:T], xh[:, k, 0:T].bitcast(F32), ALU.subtract)\
                    .then_inc(s_ml, 1)

            def scaled_residual(p, gate, tiles, view):
                for it in range(p.n // p.body):
                    for j in range(p.body):
                        multiplied(dve, p, it, j)
                        todo = [(i, s_, part) for i in range(tiles) for s_, part in enumerate(parts(T))]
                        for n, (i, s_, part) in enumerate(todo):
                            f = tiles * (it * p.body + j) + i
                            ins = v.scalar_tensor_tensor(x[:, f, part], view(p, j, i)[:, part],
                                                         mod[:, l, gate + f, s_:s_ + 1], x[:, f, part],
                                                         ALU.mult, ALU.add)
                            if n < len(todo) - 1:
                                D1.add(ins)
                        ins.then_inc(drained[unit(p, j)[0]], 1)
                all_drained(dve, p)

            scaled_residual(q["wo"], 16, 2, lambda p, j, i: gview(p, j, T)[:, i, :])
            D1.wait()
            dve.sem_inc(s_res, 1)
            norm_dve(dve, D1, n0 + 2, gain_of(l, 1), sqr2, dg2, shift=shift_of(l, 24))
            for half in range(2):
                for i in range(1 + half):
                    p, f0 = q["f1", half, i], ffn_pair0(l, half, i)
                    t0 = 4 * 2 * i if half else 0
                    for it in range(p.n // p.body):
                        for j in range(0, p.body, 2):
                            pair, s_ = f0 + 2 * it + j // 2, (j // 2) % 2
                            dve.wait_ge(s_ft, pair + 1)
                            step(v.tensor_scalar(two(pr2, s_, T), two(th2, s_, T), 0.5, 0.5, ALU.mult, ALU.add))
                            v.tensor_tensor(two(pr2, s_, T), two(pr2, s_, T), gview(p, j, T), ALU.mult)\
                                .then_inc(drained[unit(p, j)[0]], 1)
                            wait_drained(dve, p, it, j, 1)
                            multiplied(dve, p, it, j + 1)
                            step(v.tensor_tensor(two(pr2, s_, T), two(pr2, s_, T), gview(p, j + 1, T), ALU.mult))
                            dve.sem_inc(drained[unit(p, j + 1)[0]], 1)
                            dve.sem_inc(s_fp, 1)
                            dve.wait_ge(s_fh, pair + 1)
                            t = t0 + 4 * it + j
                            v.tensor_tensor(fhl[:, t:t + 2, 0:T], two(pr2, s_, T), fhh[:, t:t + 2, 0:T].bitcast(F32),
                                            ALU.subtract).then_inc(s_fl, 1)
                scaled_residual(q["f2", half], 40, 1, lambda p, j, i: unit_view(p, j, T))
            D1.wait()
            dve.sem_inc(s_res, 1)

        def back_dve(dve, l, b):
            T = layer_T(l)
            n = (BRN[l][b] - 1) * 4
            for f in range(4):
                dve.wait_ge(s_brh, n + f + 1)
                hi = brh[:, f, 0:T].bitcast(F32)
                if b == 3:
                    ins = nc.vector.scalar_tensor_tensor(brl[:, f, 0:T], mb[:, f, 0:T], dgain[:, l:l + 1], hi,
                                                         ALU.mult, ALU.subtract)
                else:
                    ins = nc.vector.tensor_tensor(brl[:, f, 0:T], mb[:, f, 0:T], hi, ALU.subtract)
                ins.then_inc(s_brl, 1)

        @block.scalar
        def _(act):
            A1 = Tally(act, s_act)
            act.dma_start(h32[:, :, :], A["x"][0].rearrange("(c j) d -> c j d", j=CH)).then_inc(s_h32, 16)
            for ri, name in enumerate(("ssm_c_re", "ssm_c_im")):
                c5 = A[name][0].rearrange("(r q g) h p -> r g q h p", r=4, g=2)
                for r in range(4):
                    for g in range(2):
                        act.dma_start(cnat[:, ri, r, 64 * g:64 * g + 64], c5[r, g]).then_inc(s_cnat, 16)
            act.dma_start(xnat[:, :, :], A["x"][0].rearrange("(a p) d -> p a d", p=P)).then_inc(s_xnat, 16)
            act.dma_start(gainb[:, :], A["norm_mix"][0, :].partition_broadcast(NCH)).then_inc(s_bd, 16)
            act.dma_start(Db, A["ssm_d"][0].rearrange("(k g h) -> k g h", k=4, h=GH)
                          .partition_broadcast(GH)).then_inc(s_bd, 16)
            for ri, name in enumerate(("ssm_b_re", "ssm_b_im")):
                act.dma_start(Bn[:, ri, :, :], A[name][0].rearrange("(q g) p h -> (g p) q h", g=2))\
                    .then_inc(s_bd, 16)
            act.wait_ge(s_pt, 1)
            nc.scalar.copy(sm[:, 0:3, :], mb[:, 1, 0:96].rearrange("p (a q) -> p a q", a=3)).then_inc(s_params, 1)
            act.wait_ge(s_params, 1)
            A1.add(nc.scalar.activation(sm[:, 3, :], sm[:, 2, :], ACT.Exp))
            A1.wait()
            act.sem_inc(s_dt, 1)
            nc.scalar.copy(vecs[:, :], mb[:, 0, :]).then_inc(s_params, 1)
            nc.scalar.copy(Ct[:, 0, :, :], mb[:, 2, :].rearrange("p (q h) -> p q h", h=GH)).then_inc(s_params, 1)
            nc.scalar.mul(Ct[:, 1, :, :], mb[:, 3, :].rearrange("p (q h) -> p q h", h=GH), -1.0).then_inc(s_params, 1)
            act.wait_ge(s_params, 4)
            A1.add(nc.scalar.activation(sc[:, :, 0:1], vecs[:, V_C:V_C + 8].rearrange("p (k o) -> p k o", o=1),
                                        ACT.Tanh, scale=0.5))
            A1.add(nc.scalar.activation(sc[:, :, 1:2], vecs[:, V_CC:V_CC + 8].rearrange("p (k o) -> p k o", o=1),
                                        ACT.Tanh, scale=0.5))
            act.wait_ge(s_ang, 1)
            A1.add(nc.scalar.activation(sm[:, 6, :], sm[:, 4, :], ACT.Exp))
            A1.add(nc.scalar.activation(sm[:, 7, :], sm[:, 5, :], ACT.Sin))
            A1.add(nc.scalar.activation(sm[:, 8, :], sm[:, 5, :], ACT.Sin, scale=0.5))
            A1.wait()
            act.sem_inc(s_sin, 1)
            act.wait_ge(s_h32, 16)
            for j in range(CH):
                if j:
                    A1.wait()
                A1.add(nc.scalar.activation(sq32[:, :], h32[:, j, :], ACT.Square, accum_out=sst[:, 0, j:j + 1]))
            A1.wait()
            act.sem_inc(s_ss, 1)
            act.wait_ge(s_xt, 1)
            nc.scalar.copy(x[:, :, 0:SEQ], gb[:, :, :].rearrange("p b (k t) -> p (b k) t", k=2)).then_inc(s_x1, 1)
            act.wait_ge(s_pw, 1)
            for j in range(CH):
                A1.add(nc.scalar.copy(pwr[:, j, :, :], pw[:, CH - 1 - j, :, :]))
            A1.wait()
            act.sem_inc(s_pwr, 1)

            def ada_copy(it, c):
                act.wait_ge(ada_used, it * 4 + (c + 1))
                if c + it_min(it) >= 2:
                    act.wait_ge(s_at, it * 4 + (c - 1))
                nc.scalar.copy(adat[:, c % 2, :], gb[0:2, 3, 0:256]).then_inc(s_ac, 1)
            for j in range(4):
                ada_copy(0, j)
            act.wait_ge(s_U, 1)
            nc.scalar.copy(U[:, :, :], mb[:, :, :].rearrange("p b (g c) -> p (b g) c", c=NCH)).then_inc(s_Uc, 1)
            for q in range(PAIRS):
                act.wait_ge(s_w1t, q + 1)
                if q >= 4:
                    act.wait_ge(s_w1u, q - 3)
                nc.scalar.copy(w1[:, q % 4, :, :], gb[:, 1 + q % 2, 0:256].rearrange("p (r m) -> p r m", r=2))\
                    .then_inc(s_w1, 1)
                if q % 2:
                    ada_copy(0, 4 + q // 2)
            act.wait_ge(s_w1u, PAIRS)
            nc.scalar.copy(V[:, :, :, :].rearrange("p c r q -> p q r c"),
                           mb[:, :, :].rearrange("p b (q r c) -> p (b q) r c", r=2, c=NCH)).then_inc(s_Vc, 1)
            act.wait_ge(s_T0, 1)
            for r in range(8):
                act.wait_ge(s_K, r + 1)
                if r == 4:
                    act.wait_ge(s_T, 16 * CH)
                g0_ = 8 * (r % 4)
                nc.scalar.copy(ksb[:, g0_:g0_ + 8, :].rearrange("p (g b) m -> p g b m", b=2),
                               mb[0:GH, 2 * (r % 2):2 * (r % 2) + 2, :].rearrange("p b (g m) -> p g b m", m=P))\
                    .then_inc(s_Kc, 1)
                if r % 4 == 3:
                    act.wait_ge(s_Kd, r + 1)
                    for ji in range(CH):
                        act.dma_start(toep[GH * ji:GH * ji + GH, 32 * (r // 4):32 * (r // 4) + 32, GH * ji:P],
                                      ksb[:, :, 0:P - GH * ji]).then_inc(s_T, 16)
                ada_copy(0, 20 + r)
            with act.Fori(1, 6) as it:
                for j in range(4):
                    ada_copy(it, 24 + j)

            def gelu_a(d):
                act.wait_ge(s_Yt, d + 1)
                if d >= 2:
                    act.wait_ge(s_xl, d - 1)
                nc.scalar.copy(gl[:, d % 2, 0, :], yview(d)).then_inc(s_y, 1)
                nc.scalar.activation(gl[:, d % 2, 1, :], yview(d), ACT.Square).then_inc(s_y2, 1)

            def gelu_b(d):
                act.wait_ge(s_yw, d + 1)
                nc.scalar.activation(gl[:, d % 2, 2, :], gl[:, d % 2, 1, :], ACT.Tanh, scale=0.7978845608028654)\
                    .then_inc(s_yt, 1)
                act.wait_ge(s_yg, d + 1)
                nc.scalar.copy(xh[:, d, 0:SEQ], gl[:, d % 2, 3, :]).then_inc(s_xh, 1)

            for d in range(KD):
                act.wait_ge(s_Y, d + 1)
                if d >= 2:
                    act.wait_ge(s_Yt, d - 1)
                for b in range(2):
                    nc.scalar.copy(ysb[:, d % 2, :, b::2, :].rearrange("p j g h -> p g j h"),
                                   mb[0:NCH, 2 * (d % 2) + b, :].rearrange("p (g j h) -> p g j h", j=CH, h=GH))\
                        .then_inc(s_Yc, 1)
                if d:
                    gelu_a(d - 1)
                    gelu_b(d - 1)
            gelu_a(KD - 1)
            gelu_b(KD - 1)

            act.wait_ge(s_Y, KD)
            for j in range(2):
                for h in range(2):
                    split_hi(act, (p_glu, 0, j), h)
            gemm_act(act, p_glu, pair_tanh(act, p_glu, SEQ))
            act.wait_ge(s_res, 1)
            norm_act(act, 0, lambda k: x[:, k, 0:SEQ], sqr)
            operand_act(act, 0, sqr)

            def relu(it, j):
                multiplied(act, p_m1, it, j)
                nc.scalar.activation(two(th, j % 2, SEQ), gview(p_m1, j, SEQ), ACT.Relu)\
                    .then_inc(drained[unit(p_m1, j)[0]], 1)
                act.wait_ge(s_r, 4 * it + (j + 1))
                nc.scalar.copy(hidh[:, bass.ds(it * 8 + 2 * j, 2), :], two(pr, j % 2, SEQ)).then_inc(s_rq, 1)
            gemm_act(act, p_m1, relu)
            gemm_act(act, p_m2, lambda it, j: None)
            act.wait_ge(s_res, 2)
            norm_act(act, 1, lambda k: x[:, k, 0:SEQ], sqr)
            operand_act(act, 1, sqr)

            act.dma_start(pnat[:, :, :], A["p"][0, 0].rearrange("(a p) d -> p a d", p=P)).then_inc(s_p, 16)
            act.wait_ge(s_pn, 1)
            nc.scalar.copy(pth[:, :, :], mb[:, 3, :].rearrange("p (k t) -> p k t", k=2)).then_inc(s_ph, 1)
            gemm_act(act, p_pl, pair_tanh(act, p_pl, SEQ))
            act.wait_ge(s_res, 3)
            norm_act(act, 2, lambda k: x[:, k, 0:SEQ], sqr)

            act.wait_ge(s_squ, sq0[3])
            act.dma_start(cxnat[:, :, :], A["ctx_2"][0].rearrange("(a p) d -> p a d", p=P)).then_inc(s_cx, 16)
            for k, name in enumerate(("q_norm_2", "k_norm_2")):
                act.dma_start(qkg[:, :, k, :], A[name].partition_broadcast(P)).then_inc(s_qkg, 16)
            for k, name in enumerate(("lam_q1_2", "lam_k1_2", "lam_q2_2", "lam_k2_2")):
                act.dma_start(lamv[:, k, :].rearrange("p (l n) -> p l n", l=LAYERS),
                              A[name].partition_broadcast(P)).then_inc(s_qkg, 16)
            act.wait_ge(s_cxt, 1)
            nc.scalar.copy(x[:, :, SEQ:SEQ + CTX], gb[:, :, :].rearrange("p b (k t) -> p (b k) t", k=2))\
                .then_inc(s_cxc, 1)
            act.wait_ge(s_lm, 1)
            nc.scalar.activation(st[:, 0, 4:8], st[:, 0, 0:4], ACT.Exp).then_inc(s_le, 1)
            act.wait_ge(s_cxc, 1)
            act.wait_ge(s_res, 4)
            for l in range(LAYERS):
                layer_act(act, l)
            act.wait_ge(s_res, RES_END - 1)
            norm_act(act, 9, lambda k: x[:, k, 0:SEQ], sqr2)
            for a in range(2):
                act.wait_ge(s_ot, a + 1)
                nc.scalar.copy(onat[:, a, :], mb[:, 2 * a:2 * a + 2, :].rearrange("p b n -> p (b n)")).then_inc(s_oc, 1)
                act.wait_ge(s_oc, a + 1)
                act.dma_start(out[0, a * P:(a + 1) * P, :], onat[:, a, :]).then_inc(s_out, 16)

        @block.gpsimd
        def _(pool):
            nc.gpsimd.memset(vnat[:, :, :], 0.0).then_inc(s_vz, 1)
            nc.gpsimd.memset(ones[:, :], 1.0).then_inc(s_ones, 1)
            P1 = Tally(pool, s_pool)
            pool.wait_ge(s_pwr, 1)
            pool.wait_ge(s_Bb, 1)
            pool.wait_ge(s_xt, 1)
            pool.wait_ge(s_ss, 1)
            for r in range(8):
                q = slice(4 * r, 4 * r + 4)
                pj = [pwr[:, :, ri, q].rearrange("p j q -> p q j").unsqueeze(3).to_broadcast([P, 4, CH, GH])
                      for ri in range(2)]
                bh = [Bb[:, ri, q, :].unsqueeze(2).to_broadcast([P, 4, CH, GH]) for ri in range(2)]
                tmp = tF[:, 0:4 * CH * GH].rearrange("p (q j h) -> p q j h", q=4, h=GH)
                if r >= 2:
                    pool.wait_ge(s_w1t, 4 * (r - 1))
                for ri, op in ((0, ALU.subtract), (1, ALU.add)):
                    Fr = F[:, r % 2, :, ri, :, :]
                    P1.add(nc.gpsimd.tensor_tensor(Fr, pj[0], bh[ri], ALU.mult))
                    P1.add(nc.gpsimd.tensor_tensor(tmp, pj[1], bh[1 - ri], ALU.mult))
                    P1.wait()
                    ins = nc.gpsimd.tensor_tensor(Fr, Fr, tmp, op)
                    if ri == 0:
                        P1.add(ins)
                        P1.wait()
                ins.then_inc(s_F, 1)
                pool.wait_ge(s_F, r + 1)
            pool.wait_ge(s_U, 1)
            nc.gpsimd.memset(toep[:, :, :], 0.0).then_inc(s_T0, 1)

            for p in phases[2:]:
                def turn(it, p=p):
                    for j in range(p.body):
                        m = p.m0 + j
                        for h in range(2):
                            pool.wait_ge(hi_ready, it * (2 * p.body) + (2 * m + h + 1))
                            nc.gpsimd.tensor_tensor(split_half(wl, p, j, h), raw_half(p, j, h),
                                                    split_half(wh, p, j, h).bitcast(F32), ALU.subtract)\
                                .then_inc(w_ready, 1)
                repeat(pool, p.n // p.body, turn)

        def gemm_pe(pe, p, T, X, need=None):
            def turn(it):
                for j in range(p.body):
                    m = p.m0 + j
                    kb = j % p.units
                    kt = p.kts[j]
                    if kb == 0:
                        wait_drained(pe, p, it, j)
                    g = gview(p, j, T)
                    for b in range(2):
                        pe.wait_ge(w_ready, it * (2 * p.body) + (2 * m + b + 1))
                        H, L = split_half(wh, p, j, b), split_half(wl, p, j, b)
                        for k in range(kt):
                            if need is not None and b == 0:
                                need(it, j, k)
                            XH, XL = X(j, kb * kt + k)
                            st, sp_ = kb == 0 and k == 0, kb == p.units - 1 and k == kt - 1
                            nc.tensor.matmul(g[:, b, :], H[:, k, :], XH, start=st, stop=False)
                            nc.tensor.matmul(g[:, b, :], H[:, k, :], XL, start=False, stop=False)
                            ins = nc.tensor.matmul(g[:, b, :], L[:, k, :], XH, start=False, stop=sp_)
                        ins.then_inc(mm_done, 1)

            repeat(pe, p.n // p.body, turn, peel_first=True)

        @block.tensor
        def _(pe):
            pe.wait_ge(s_const, 16)
            pe.wait_ge(s_nat, 16 * NAT_SP)
            for a in range(3):
                nc.tensor.transpose(mb[:, 1, 32 * a:32 * a + 32], lnat[:, a, :], ident[0:PAIRS, 0:PAIRS]) \
                    if a < 2 else None
            pe.wait_ge(s_ldt, 1)
            nc.tensor.transpose(mb[:, 1, 64:96], lnat[:, 2, :], ident[0:PAIRS, 0:PAIRS])
            for a in range(4):
                nc.tensor.transpose(mb[:, 0, a * P:a * P + P], vnat[:, a, :], ident)
            pe.wait_ge(s_cnat, 16 * 16)
            for ri in range(2):
                for r in range(4):
                    ins = nc.tensor.transpose(mb[:, 2 + ri, r * P:r * P + P], cnat[:, ri, r, :], ident)
            ins.then_inc(s_pt, 1)
            pe.wait_ge(s_xnat, 16)
            for k in range(KD):
                for a in range(2):
                    ins = nc.tensor.transpose(gb[:, k // 2, (k % 2) * 256 + a * P:(k % 2) * 256 + a * P + P],
                                              xnat[:, a, k * P:k * P + P], ident)
            ins.then_inc(s_xt, 1)

            def ada_transposes(it, c):
                pe.wait_ge(s_ac, it * 4 + (c + 1))
                for b in range(2):
                    ins = nc.tensor.matmul(gb[:, 0, bass.ds(it * 16 + (4 * c + 2 * b), 2)],
                                              adat[:, c % 2, b * P:b * P + P], ident[0:2, 0:2], start=True, stop=True)
                ins.then_inc(s_at, 1)

            def ada_block(l, it, j):
                p, c = ada[l], 24 * l + j
                has_landed(pe, p, it, j)
                if c + it_min(it):
                    pe.wait_ge(s_ac, it * 4 + c)
                W = rawv((p.g0 + j) % RING, KD)
                for k in range(KD):
                    ins = nc.tensor.matmul(gb[0:2, 3, 0:256], sc[:, k, :], W[:, k, :],
                                           start=(k == 0), stop=(k == KD - 1))
                ins.then_inc(ada_used, 1)
                if c + it_min(it):
                    ada_transposes(it, c - 1)

            pe.wait_ge(s_sc, 1)
            pe.wait_ge(s_x1, 1)
            for j in range(4):
                ada_block(0, 0, j)
            pe.wait_ge(s_h, 1)
            pe.wait_ge(s_params, 4)
            for g in range(GROUPS):
                ins = nc.tensor.transpose(mb[:, g // 16, (g % 16) * NCH:(g % 16) * NCH + NCH],
                                          hn[:, g, :, :], ident[0:NCH, 0:NCH])
            ins.then_inc(s_U, 1)

            def w1_transposes(q):
                if q % 4 == 0:
                    pe.wait_ge(s_F, q // 4 + 1)
                if q >= 2:
                    pe.wait_ge(s_w1, q - 1)
                for ri in range(2):
                    ins = nc.tensor.transpose(gb[:, 1 + q % 2, ri * P:ri * P + P],
                                              F[:, (q // 4) % 2, q % 4, ri, :, :], ident)
                ins.then_inc(s_w1t, 1)

            def v_products(q):
                pe.wait_ge(s_w1, q + 1)
                for ri in range(2):
                    for g in range(2):
                        c = (q % 8) * 64 + ri * 32
                        ins = nc.tensor.matmul(mb[64 * g:64 * g + 64, q // 8, c:c + NCH],
                                               w1[:, q % 4, ri, 64 * g:64 * g + 64], U[:, 2 * q + g, :],
                                               start=True, stop=True)
                ins.then_inc(s_w1u, 1)

            pe.wait_ge(s_Uc, 1)
            for q in range(PAIRS + 1):
                if q < PAIRS:
                    w1_transposes(q)
                if q:
                    v_products(q - 1)
                if q % 2 and q < PAIRS:
                    ada_block(0, 1 + q // 8, (q // 2) % 4)
            pe.wait_ge(s_Vc, 1)
            for r in range(8):
                if r % 2 == 0:
                    pe.wait_ge(s_E, r // 2 + 1)
                if r >= 2:
                    pe.wait_ge(s_Kc, r - 1)
                for gg in range(8):
                    g = 8 * r + gg
                    q, h = g // 2, slice(64 * (g % 2), 64 * (g % 2) + 64)
                    o = mb[0:GH, 2 * (r % 2) + gg % 2, (gg // 2) * P:(gg // 2) * P + P]
                    nc.tensor.matmul(o, Bb[h, 0, q, :], E[h, q, 0, 0:CH, :], start=True, stop=False)
                    ins = nc.tensor.matmul(o, Bb[h, 1, q, :], E[h, q, 1, 0:CH, :], start=False, stop=True)
                ins.then_inc(s_K, 1)
                ada_block(*((0, 5, r) if r < 4 else (1, 0, r - 4)))
            with pe.Fori(1, 6) as it:
                for j in range(4):
                    ada_block(1, it, j)
            ada_transposes(0, 47)
            pe.wait_ge(s_S, 1)
            pe.wait_ge(s_T, 16 * CH * 2)
            pe.wait_ge(s_Kc, 8)

            def y_products(d):
                if d >= 2:
                    pe.wait_ge(s_Yc, 2 * (d - 1))
                for gg in range(8):
                    g = 8 * d + gg
                    q, h = g // 2, slice(64 * (g % 2), 64 * (g % 2) + 64)
                    o = mb[0:NCH, 2 * (d % 2) + gg % 2, (gg // 2) * P:(gg // 2) * P + P]
                    nc.tensor.matmul(o, U[:, g, :], toep[:, g, :], start=True, stop=False)
                    nc.tensor.matmul(o, S[h, :, 0, q], E[h, q, 0, 1:CH + 1, :], start=False, stop=False)
                    ins = nc.tensor.matmul(o, S[h, :, 1, q], E[h, q, 1, 1:CH + 1, :], start=False, stop=True)
                ins.then_inc(s_Y, 1)

            def y_transposes(d):
                pe.wait_ge(s_Yc, 2 * (d + 1))
                if d >= 2:
                    pe.wait_ge(s_y2, d - 1)
                o = yview(d).rearrange("p (c j) -> p c j", j=CH)
                for j in range(CH):
                    ins = nc.tensor.transpose(o[:, :, j], ysb[:, d % 2, j, :, :], ident[0:NCH, 0:NCH])
                ins.then_inc(s_Yt, 1)

            for d in range(KD + 1):
                if d < KD:
                    y_products(d)
                if d:
                    y_transposes(d - 1)

            pe.wait_ge(s_mod, 1)
            X = lambda j, k: (xh[:, k, 0:SEQ], xl[:, k, 0:SEQ])

            def operand(n):
                def need(it, j, k):
                    if j == 0 and it_min(it) == 0 and isinstance(it, int):
                        pe.wait_ge(s_xl, 8 * n + k + 1)
                return need
            gemm_pe(pe, p_glu, SEQ, X, operand(0))
            norm_pe(pe, 0, sqr, diag)
            gemm_pe(pe, p_m1, SEQ, X, operand(1))

            def hidden(it, j, k):
                if k == 0 and isinstance(it, int):
                    pe.wait_ge(s_hl, 4 * (j % 4) + 4)
            gemm_pe(pe, p_m2, SEQ, lambda j, k: (hidh[:, k, :], hidl[:, k, :]), hidden)
            norm_pe(pe, 1, sqr, diag)
            pe.wait_ge(s_p, 16)
            for k in range(2):
                for a in range(2):
                    ins = nc.tensor.transpose(mb[:, 3, k * 256 + a * P:k * 256 + a * P + P],
                                              pnat[:, a, k * P:k * P + P], ident)
            ins.then_inc(s_pn, 1)

            def operand_p(it, j, k):
                if isinstance(it, int) and it == 0:
                    if j == 0:
                        pe.wait_ge(s_xl, 16 + k + 1)
                    if j == 1 and k == 0:
                        pe.wait_ge(s_pl, 1)
            gemm_pe(pe, p_pl, SEQ, lambda j, k: (pth[:, k, :], ptl[:, k, :]) if j % 2 else X(j, k), operand_p)
            norm_pe(pe, 2, sqr, diag)
            pe.wait_ge(s_cx, 16)
            all_drained(pe, p_pl)
            for k in range(KD):
                for a in range(2):
                    ins = nc.tensor.transpose(gb[:, k // 2, (k % 2) * 256 + a * P:(k % 2) * 256 + a * P + P],
                                              cxnat[:, a, k * P:k * P + P], ident)
            ins.then_inc(s_cxt, 1)
            pe.wait_ge(s_cxc, 1)
            for l in range(LAYERS):
                layer_pe(pe, l)
            norm_pe(pe, 9, sqr2, dg2)
            pe.wait_ge(s_res, RES_END)
            for a in range(2):
                for k in range(KD):
                    ins = nc.tensor.transpose(mb[:, 2 * a + k // 4, (k % 4) * P:(k % 4) * P + P],
                                              x[:, k, a * P:a * P + P], ident)
                ins.then_inc(s_ot, 1)

        @block.vector
        def _(dve):
            D1 = Tally(dve, s_dve)
            v = nc.vector

            def step(ins):
                D1.add(ins)
                D1.wait()

            def cmul(dr, di, ar, ai, br, bi, tmp):
                D1.add(v.tensor_tensor(dr, ar, br, ALU.mult))
                step(v.tensor_tensor(tmp, ai, bi, ALU.mult))
                D1.add(v.tensor_tensor(dr, dr, tmp, ALU.subtract))
                step(v.tensor_tensor(di, ar, bi, ALU.mult))
                step(v.tensor_tensor(tmp, ai, br, ALU.mult))
                step(v.tensor_tensor(di, di, tmp, ALU.add))

            dve.wait_ge(s_nat, 16 * NAT_SP)
            v.tensor_copy(lnat[:, 2, :].rearrange("p (g s) -> p g s", g=2),
                          lnat[:, 3, 0:2].unsqueeze(2).to_broadcast([PAIRS, 2, STATE])).then_inc(s_ldt, 1)
            dve.wait_ge(s_dt, 1)
            lr, li, dt = sm[:, 0, :], sm[:, 1, :], sm[:, 3, :]
            D1.add(v.tensor_tensor(sm[:, 4, :], lr, dt, ALU.mult))
            step(v.tensor_tensor(sm[:, 9, :], li, dt, ALU.mult))
            big = 12582912.0
            step(v.tensor_scalar(sm[:, 10, :], sm[:, 9, :], float(1 / (2 * np.pi)), big, ALU.mult, ALU.add))
            step(v.tensor_scalar(sm[:, 10, :], sm[:, 10, :], big, None, ALU.subtract))
            turn = 2 * np.pi
            c1 = 6.28125
            c2 = float(np.floor((turn - c1) * 2 ** 20) / 2 ** 20)
            c3 = turn - c1 - c2
            src = sm[:, 9, :]
            for cc in (c1, c2, c3):
                step(v.scalar_tensor_tensor(sm[:, 5, :], sm[:, 10, :], -cc, src, ALU.mult, ALU.add))
                src = sm[:, 5, :]
            step(v.tensor_scalar(sm[:, 5, :], sm[:, 5, :], 3.1415925, -3.1415925, ALU.min, ALU.max))
            dve.sem_inc(s_ang, 1)
            dve.wait_ge(s_sin, 1)
            for s in range(2):
                o = V_C + 8 * s
                step(v.tensor_scalar(sc[:, :, s], sc[:, :, s], 0.5, 0.5, ALU.mult, ALU.add))
                step(v.tensor_tensor(sc[:, :, s], sc[:, :, s], vecs[:, o:o + 8], ALU.mult))
            dve.sem_inc(s_sc, 1)
            step(v.tensor_tensor(sm[:, 11, :], sm[:, 8, :], sm[:, 8, :], ALU.mult))
            step(v.tensor_scalar(sm[:, 11, :], sm[:, 11, :], -2.0, 1.0, ALU.mult, ALU.add))
            D1.add(v.tensor_tensor(pw[:, 1, 0, :], sm[:, 6, :], sm[:, 11, :], ALU.mult))
            D1.add(v.memset(pw[:, 0, 0, :], 1.0))
            D1.add(v.memset(pw[:, 0, 1, :], 0.0))
            step(v.tensor_tensor(pw[:, 1, 1, :], sm[:, 6, :], sm[:, 7, :], ALU.mult))
            for n, lo in ((1, 2), (2, 3), (4, 5)):
                k = lo - 1 if n == 1 else n
                fac = [pw[:, k, ri, :].unsqueeze(1).to_broadcast([P, n, PAIRS]) for ri in range(2)]
                tmp = sm[:, 12:12 + n, :]
                cmul(pw[:, lo:lo + n, 0, :], pw[:, lo:lo + n, 1, :], pw[:, 1:1 + n, 0, :], pw[:, 1:1 + n, 1, :],
                     fac[0], fac[1], tmp)
            dve.sem_inc(s_pw, 1)
            ni = pw[:, 1, 1, :]
            D1.add(v.tensor_scalar(sm[:, 12, :], pw[:, 1, 0, :], -1.0, None, ALU.add))
            D1.add(v.tensor_tensor(sm[:, 13, :], lr, lr, ALU.mult))
            step(v.tensor_tensor(sm[:, 14, :], li, li, ALU.mult))
            D1.add(v.tensor_tensor(sm[:, 15, :], sm[:, 12, :], lr, ALU.mult))
            D1.add(v.tensor_tensor(sm[:, 16, :], ni, li, ALU.mult))
            D1.add(v.tensor_tensor(sm[:, 17, :], ni, lr, ALU.mult))
            D1.add(v.tensor_tensor(sm[:, 18, :], sm[:, 12, :], li, ALU.mult))
            step(v.tensor_tensor(sm[:, 13, :], sm[:, 13, :], sm[:, 14, :], ALU.add))
            D1.add(v.reciprocal(sm[:, 19, :], sm[:, 13, :]))
            D1.add(v.tensor_tensor(sm[:, 15, :], sm[:, 15, :], sm[:, 16, :], ALU.add))
            step(v.tensor_tensor(sm[:, 17, :], sm[:, 17, :], sm[:, 18, :], ALU.subtract))
            D1.add(v.tensor_tensor(sm[:, 15, :], sm[:, 15, :], sm[:, 19, :], ALU.mult))
            step(v.tensor_tensor(sm[:, 17, :], sm[:, 17, :], sm[:, 19, :], ALU.mult))
            dve.wait_ge(s_bd, 64)
            dve.wait_ge(s_xt, 1)
            dve.wait_ge(s_ss, 1)
            cf = [sm[:, k, :].unsqueeze(2).to_broadcast([P, PAIRS, GH]) for k in (15, 17)]
            tmp = tE[:, 0:PAIRS * GH].rearrange("p (q h) -> p q h", h=GH)
            cmul(Bb[:, 0, :, :], Bb[:, 1, :, :], Bn[:, 0, :, :], Bn[:, 1, :, :], cf[0], cf[1], tmp)
            dve.sem_inc(s_Bb, 1)
            rsqrt(D1, sst[:, 1, :], sst[:, 2, :], sst[:, 3, :], sst[:, 0, :], sst[:, 0, :], 1.0 / D, EPS)
            for j in range(CH):
                D1.add(v.scalar_tensor_tensor(hn[:, :, j, :], h32[:, j, :].rearrange("p (g h) -> p g h", h=GH),
                                              sst[:, 2, j:j + 1], gainb[:, :].rearrange("p (g h) -> p g h", h=GH),
                                              ALU.mult, ALU.mult))
            D1.wait()
            dve.sem_inc(s_h, 1)
            dve.wait_ge(s_params, 4)
            for r in range(4):
                q = slice(8 * r, 8 * r + 8)
                pj = [pw[:, :, ri, q].rearrange("p j q -> p q j").unsqueeze(3).to_broadcast([P, 8, CH + 1, GH])
                      for ri in range(2)]
                ch = [Ct[:, ri, q, :].unsqueeze(2).to_broadcast([P, 8, CH + 1, GH]) for ri in range(2)]
                tmp = tE[:, :].rearrange("p (q j h) -> p q j h", q=8, h=GH)
                for ri, op in ((0, ALU.add), (1, ALU.subtract)):
                    D1.add(v.tensor_tensor(E[:, q, ri, :, :], pj[0], ch[ri], ALU.mult))
                    step(v.tensor_tensor(tmp, pj[1], ch[1 - ri], ALU.mult))
                    step(v.tensor_tensor(E[:, q, ri, :, :], E[:, q, ri, :, :], tmp, op))
                dve.sem_inc(s_E, 1)
            step(v.tensor_tensor(Db, Db, const[0:GH, C_EYE:C_END].unsqueeze(1).unsqueeze(1)
                                 .to_broadcast([GH, 4, 16, GH]), ALU.mult))
            D1.add(v.tensor_copy(tS[:, 0, :, :], pw[:, CH, 0, :].unsqueeze(1).to_broadcast([P, 2, PAIRS])))
            D1.add(v.tensor_scalar(tS[:, 1, 0, :], pw[:, CH, 1, :], -1.0, None, ALU.mult))
            D1.add(v.tensor_copy(tS[:, 1, 1, :], pw[:, CH, 1, :]))
            step(v.memset(S[:, 0, :, :], 0.0))
            dve.wait_ge(s_Vc, 1)
            with dve.Fori(0, NCH - 1) as c, D1.loop(c, NCH - 1, 5):
                cur, nxt = S[:, bass.ds(c, 1), :, :], S[:, bass.ds(c + 1, 1), :, :]
                D1.add(v.tensor_tensor(tS[:, 2:3, 0, :], cur[:, :, 1, :], tS[:, 1:2, 0, :], ALU.mult))
                D1.add(v.tensor_tensor(tS[:, 2:3, 1, :], cur[:, :, 0, :], tS[:, 1:2, 1, :], ALU.mult))
                step(v.tensor_tensor(nxt, cur, tS[:, 0:1, :, :], ALU.mult))
                step(v.tensor_tensor(nxt, nxt, V[:, bass.ds(c, 1), :, :], ALU.add))
                step(v.tensor_tensor(nxt, nxt, tS[:, 2:3, :, :], ALU.add))
            dve.sem_inc(s_S, 1)
            for r in range(8):
                dve.wait_ge(s_Kc, r + 1)
                g0_ = 8 * (r % 4)
                v.tensor_tensor(ksb[:, g0_:g0_ + 8, 0:GH], ksb[:, g0_:g0_ + 8, 0:GH],
                                Db[:, r // 2, 8 * (r % 2):8 * (r % 2) + 8, :], ALU.add).then_inc(s_Kd, 1)
            dve.wait_ge(s_at, 48)

            for l in range(LAYERS):
                D1.add(v.tensor_tensor(mod[:, l, :, :],
                                       gb[:, 0, 96 * l:96 * l + 96].rearrange("p (c s) -> p c s", s=2),
                                       vecs[:, V_BADA + 48 * l:V_BADA + 48 * l + 48].unsqueeze(2)
                                       .to_broadcast([P, 48, 2]), ALU.add))
            D1.wait()
            dve.sem_inc(s_mod, 1)
            for l in range(LAYERS):
                for k, (ch, gv) in enumerate(((8, V_NMIX2), (32, V_NFFN2))):
                    step(v.tensor_scalar(msc[:, l, k, :, :], mod[:, l, ch:ch + 8, :], 1.0, None, ALU.add))
                    step(v.tensor_tensor(msc[:, l, k, :, :], msc[:, l, k, :, :],
                                         vecs[:, gv + 8 * l:gv + 8 * l + 8].unsqueeze(2).to_broadcast([P, KD, 2]),
                                         ALU.mult))
            for d in range(KD):
                y, w, t, g = (gl[:, d % 2, k, :] for k in range(4))
                dve.wait_ge(s_y2, d + 1)
                step(v.tensor_scalar(w, w, 0.044715, 1.0, ALU.mult, ALU.add))
                v.tensor_tensor(w, w, y, ALU.mult).then_inc(s_yw, 1)
                dve.wait_ge(s_yt, d + 1)
                step(v.tensor_scalar(t, t, 0.5, 0.5, ALU.mult, ALU.add))
                v.tensor_tensor(g, t, y, ALU.mult).then_inc(s_yg, 1)
                dve.wait_ge(s_xh, d + 1)
                v.tensor_tensor(xl[:, d, 0:SEQ], g, xh[:, d, 0:SEQ].bitcast(F32), ALU.subtract).then_inc(s_xl, 1)

            def gated_residual(p, T):
                trips = p.n // p.body

                def turn(it):
                    for j in range(0, p.body, 2):
                        s = (j // 2) % 2
                        wait_drained(dve, p, it, j, 1)
                        step(v.tensor_scalar(two(pr, s, T), two(th, s, T), 0.5, 0.5, ALU.mult, ALU.add))
                        multiplied(dve, p, it, j + 1)
                        b, n, per = unit(p, j + 1)
                        v.tensor_tensor(two(pr, s, T), two(pr, s, T), gview(p, j + 1, T), ALU.mult)\
                            .then_inc(drained[b], 1)
                        wait_drained(dve, p, it, j + 1, 1)
                        xs = x[:, bass.ds(it * p.body + j, 2), 0:T]
                        D1.add(v.tensor_tensor(xs, xs, two(pr, s, T), ALU.add))
                for it in range(trips):
                    turn(it)
                D1.wait()
                dve.sem_inc(s_res, 1)

            gated_residual(p_glu, SEQ)
            norm_dve(dve, D1, 0, vec(V_NFFN), sqr, diag)

            def hid_turn(it):
                for j in range(p_m1.body):
                    s = j % 2
                    hs = bass.ds(it * 8 + 2 * j, 2)
                    wait_drained(dve, p_m1, it, j, 1)
                    v.tensor_tensor(two(pr, s, SEQ), two(th, s, SEQ), two(th, s, SEQ), ALU.mult).then_inc(s_r, 1)
                    dve.wait_ge(s_rq, it * 4 + (j + 1))
                    v.tensor_tensor(hidl[:, hs, :], two(pr, s, SEQ), hidh[:, hs, :].bitcast(F32), ALU.subtract)\
                        .then_inc(s_hl, 1)
            repeat(dve, p_m1.n // p_m1.body, hid_turn)
            for u in range(4):
                it, j = u // 2, 4 * (u % 2)
                multiplied(dve, p_m2, it, j + 3)
                xs = x[:, 2 * u:2 * u + 2, 0:SEQ]
                v.tensor_tensor(xs, xs, gview(p_m2, j, SEQ), ALU.add).then_inc(drained[unit(p_m2, j)[0]], 1)
            for j in (0, 4):
                wait_drained(dve, p_m2, 1, j, 1)
            dve.sem_inc(s_res, 1)
            norm_dve(dve, D1, 1, vec(V_NPLE), sqr, diag)
            dve.wait_ge(s_ph, 1)
            v.tensor_tensor(ptl[:, :, :], mb[:, 3, :].rearrange("p (k t) -> p k t", k=2), pth[:, :, :].bitcast(F32),
                            ALU.subtract).then_inc(s_pl, 1)
            gated_residual(p_pl, SEQ)
            norm_dve(dve, D1, 2, vec(V_NFIN), sqr, diag, in_place=True)
            dve.sem_inc(s_res, 1)
            dve.wait_ge(s_qkg, 16 * 6)
            for k in range(2):
                step(v.tensor_tensor(lamv[:, 2 * k, :], lamv[:, 2 * k, :], lamv[:, 2 * k + 1, :], ALU.mult))
                step(v.tensor_reduce(st[:, 0, 2 * k:2 * k + 2], lamv[:, 2 * k, :].rearrange("p (l n) -> p l n", l=LAYERS),
                                     AX_X, ALU.add))
            dve.sem_inc(s_lm, 1)
            dve.wait_ge(s_le, 1)
            step(v.tensor_tensor(lamb[:, :], st[:, 0, 6:8], st[:, 0, 4:6], ALU.subtract))
            for l in range(LAYERS):
                init = 0.8 - 0.6 * float(np.exp(-0.3 * l))
                D1.add(v.tensor_scalar(lamb[:, l:l + 1], lamb[:, l:l + 1], -init, None, ALU.add))
                D1.add(v.tensor_scalar(dgain[:, l:l + 1], vecs[:, V_DN + l:V_DN + l + 1], 1.0 - init, None, ALU.mult))
            D1.wait()
            for l in range(LAYERS):
                layer_dve(dve, D1, l)
            norm_dve(dve, D1, 9, vec(V_FIN2), sqr2, dg2, in_place=True)
            dve.sem_inc(s_res, 1)


_INS = ["x", "p", "norm_mix", "norm_ffn", "norm_ple", "norm_final", "ssm_lam_re", "ssm_lam_im", "ssm_log_dt",
        "ssm_b_re", "ssm_b_im", "ssm_c_re", "ssm_c_im", "ssm_d", "ssm_w_glu", "mlp_w1", "mlp_w2", "ple_w",
        "ple_gate_w", "c_2", "ctx_2", "c_ctx_2", "w_ada_2", "b_ada_2", "norm_mix_2", "w_in_2", "w_four_2",
        "conv_w_2", "conv_b_2", "conv_ln_g_2", "conv_ln_b_2", "w_conv_2", "q_norm_2", "k_norm_2", "w_gqa_2",
        "lam_q1_2", "lam_k1_2", "lam_q2_2", "lam_k2_2", "diff_norm_2", "w_diff_2", "w_out_2", "norm_ffn_2",
        "w_ffn1_2", "w_ffn3_2", "w_ffn2_2", "final_norm_2"]


def kernel(**inputs):
    import concourse.bacc as _bacc
    from concourse.bass_utils import run_bass_kernel_spmd as _run

    nc = _bacc.Bacc("TRN2", target_bir_lowering=False, num_devices=1)
    arrays, A = {}, {}
    for name in _INS + ["consts"]:
        a = np.ascontiguousarray(shape_constants() if name == "consts" else inputs[name])
        arrays[f"in_{name}"] = a
        A[name] = nc.dram_tensor(f"in_{name}", a.shape, mybir.dt.from_np(a.dtype), kind="ExternalInput").ap()
    out = nc.dram_tensor("out_0", (1, SEQ, D), F32, kind="ExternalOutput").ap()
    build(nc, A, out)
    r = _run(nc, [arrays], core_ids=[0])
    return r.results[0]["out_0"]
```
